# Optimizing a Trainium2 kernel written in Bass

```python
import jax, jax.numpy as jnp
from jax import lax
import numpy as np

D_MODEL = 1024
BATCH = 1
SEQ = 256
DEPTH = 2

GRID_W = 64
MIX_W = D_MODEL
EPS = 1e-6
D_RNN = MIX_W
RNN_BLOCKS = 4
RNN_BW = D_RNN // RNN_BLOCKS
CONV_A_W = 4
CONV_A_LEFT = 2
LRU_C = 8.0
N_HEADS = 8
N_KV = 2
HEAD_DIM = MIX_W // N_HEADS
GROUP = N_HEADS // N_KV
ROPE_THETA = 10000.0
Q_BLOCK = 128
D_CONV = MIX_W
CONV_C_W = 3
CONV_C_LEFT = 1
N_BRANCH = 3
IN_SIZES = (D_RNN, D_RNN,
            N_HEADS * HEAD_DIM, N_KV * HEAD_DIM, N_KV * HEAD_DIM, N_HEADS * HEAD_DIM,
            D_CONV, D_CONV, D_CONV, D_CONV,
            N_BRANCH * D_MODEL)
N_IN = sum(IN_SIZES)

kernel_name = "hybrid_rglru_gqa_shortconv_encoder"

def rms_norm(x, g):
    xf = x.astype(jnp.float32)
    y = xf * lax.rsqrt(jnp.mean(xf * xf, axis=-1, keepdims=True) + EPS)
    return (y * g.astype(jnp.float32)).astype(x.dtype)

def dwconv(x, w, left):
    K = w.shape[0]
    S = x.shape[1]
    xp = jnp.pad(x, ((0, 0), (left, K - 1 - left), (0, 0)))
    y = xp[:, 0:S] * w[0]
    for k in range(1, K):
        y = y + xp[:, k:k + S] * w[k]
    return y

def _combine(e1, e2):
    a1, b1 = e1
    a2, b2 = e2
    return a1 * a2, a2 * b1 + b2

def rg_lru_dir(x, w_r, b_r, w_i, b_i, lam, reverse):
    B_, S, _ = x.shape
    xb = x.reshape(B_, S, RNN_BLOCKS, RNN_BW)
    r = jax.nn.sigmoid(jnp.einsum('bsnc,ncd->bsnd', xb, w_r).reshape(B_, S, D_RNN) + b_r)
    i = jax.nn.sigmoid(jnp.einsum('bsnc,ncd->bsnd', xb, w_i).reshape(B_, S, D_RNN) + b_i)
    log_a = -LRU_C * r.astype(jnp.float32) * jax.nn.softplus(-lam.astype(jnp.float32))
    a = jnp.exp(log_a)
    u = jnp.sqrt(-jnp.expm1(2.0 * log_a)) * (i * x).astype(jnp.float32)
    _, h = lax.associative_scan(_combine, (a, u), axis=1, reverse=reverse)
    return h

def axial_rope_tables(S):
    rows = S // GRID_W
    row = jnp.repeat(jnp.arange(rows, dtype=jnp.float32), GRID_W)
    col = jnp.tile(jnp.arange(GRID_W, dtype=jnp.float32), rows)
    half = HEAD_DIM // 2
    inv = ROPE_THETA ** (-jnp.arange(0, half, 2, dtype=jnp.float32) / half)
    ang_r = row[:, None] * inv
    ang_c = col[:, None] * inv
    return jnp.cos(ang_r), jnp.sin(ang_r), jnp.cos(ang_c), jnp.sin(ang_c)

def rope_1d(x, cos, sin):
    f = x.shape[-1] // 2
    x1, x2 = x[..., :f], x[..., f:]
    cs = cos[None, :, None, :]
    sn = sin[None, :, None, :]
    return jnp.concatenate([x1 * cs - x2 * sn, x2 * cs + x1 * sn], axis=-1)

def apply_axial_rope(x, tabs):
    cos_r, sin_r, cos_c, sin_c = tabs
    half = HEAD_DIM // 2
    xf = x.astype(jnp.float32)
    y = jnp.concatenate([rope_1d(xf[..., :half], cos_r, sin_r),
                         rope_1d(xf[..., half:], cos_c, sin_c)], axis=-1)
    return y.astype(x.dtype)

def gqa_attention(q, k, v, q_g, k_g, tabs):
    B_, S, _ = q.shape
    q = q.reshape(B_, S, N_HEADS, HEAD_DIM)
    k = k.reshape(B_, S, N_KV, HEAD_DIM)
    v = v.reshape(B_, S, N_KV, HEAD_DIM)
    q = apply_axial_rope(rms_norm(q, q_g), tabs) * (HEAD_DIM ** -0.5)
    k = apply_axial_rope(rms_norm(k, k_g), tabs)
    qb = q.reshape(B_, S // Q_BLOCK, Q_BLOCK, N_KV, GROUP, HEAD_DIM).transpose(1, 0, 2, 3, 4, 5)

    def block(qi):
        s = jnp.einsum('bqkgd,bskd->bkgqs', qi, k).astype(jnp.float32)
        p = jax.nn.softmax(s, axis=-1).astype(v.dtype)
        return jnp.einsum('bkgqs,bskd->bqkgd', p, v)

    o = lax.map(block, qb)
    return o.transpose(1, 0, 2, 3, 4, 5).reshape(B_, S, N_HEADS * HEAD_DIM)

def setup_inputs(seed: int = 0) -> dict:
    key = jax.random.key(seed)
    ks = jax.random.split(key, 20)
    f32 = jnp.float32
    nrm = lambda k, shp, s: jax.random.normal(k, shp, f32) * s
    a8 = jax.random.uniform(ks[12], (DEPTH, 2, D_RNN), f32, minval=0.9, maxval=0.999)
    a = a8 ** (1.0 / LRU_C)
    lam = jnp.log(a) - jnp.log1p(-a)
    return {
        "x": nrm(ks[0], (BATCH, SEQ, D_MODEL), 1.0),
        "c": nrm(ks[1], (BATCH, D_MODEL), 1.0),
        "w_ada": nrm(ks[2], (DEPTH, D_MODEL, 3 * D_MODEL), 0.5 * D_MODEL ** -0.5),
        "b_ada": nrm(ks[3], (DEPTH, 3 * D_MODEL), 0.01),
        "norm_g": 1.0 + nrm(ks[4], (DEPTH, D_MODEL), 0.02),
        "w_in": nrm(ks[5], (DEPTH, D_MODEL, N_IN), D_MODEL ** -0.5),
        "conv_a_w": nrm(ks[6], (DEPTH, CONV_A_W, D_RNN), CONV_A_W ** -0.5),
        "conv_a_b": nrm(ks[7], (DEPTH, D_RNN), 0.01),
        "w_rg": nrm(ks[8], (DEPTH, 2, RNN_BLOCKS, RNN_BW, RNN_BW), RNN_BW ** -0.5),
        "b_rg": nrm(ks[9], (DEPTH, 2, D_RNN), 0.01),
        "w_ig": nrm(ks[10], (DEPTH, 2, RNN_BLOCKS, RNN_BW, RNN_BW), RNN_BW ** -0.5),
        "b_ig": nrm(ks[11], (DEPTH, 2, D_RNN), 0.01),
        "lru_lam": lam,
        "q_norm_g": 1.0 + nrm(ks[13], (DEPTH, HEAD_DIM), 0.02),
        "k_norm_g": 1.0 + nrm(ks[14], (DEPTH, HEAD_DIM), 0.02),
        "conv_c_w": nrm(ks[15], (DEPTH, CONV_C_W, D_CONV), CONV_C_W ** -0.5),
        "w_branch": nrm(ks[16], (DEPTH, N_BRANCH, MIX_W, D_MODEL), MIX_W ** -0.5),
        "w_out": nrm(ks[17], (DEPTH, D_MODEL, D_MODEL), D_MODEL ** -0.5),
    }

def reference(x, c, w_ada, b_ada, norm_g, w_in, conv_a_w, conv_a_b, w_rg, b_rg, w_ig, b_ig,
              lru_lam, q_norm_g, k_norm_g, conv_c_w, w_branch, w_out):
    B_, S, D = x.shape
    tabs = axial_rope_tables(S)
    offsets = [int(o) for o in np.cumsum(IN_SIZES)[:-1]]
    for l in range(DEPTH):
        mod = c @ w_ada[l] + b_ada[l]
        shift, scale, gate = jnp.split(mod, 3, axis=-1)
        h = rms_norm(x, norm_g[l]) * (1.0 + scale[:, None, :]) + shift[:, None, :]
        proj = h @ w_in[l]
        (xa, ga, q, k, v, gb, xc, bc, cc, gc, mg) = jnp.split(proj, offsets, axis=-1)

        ua = dwconv(xa, conv_a_w[l], CONV_A_LEFT) + conv_a_b[l]
        hf = rg_lru_dir(ua, w_rg[l, 0], b_rg[l, 0], w_ig[l, 0], b_ig[l, 0], lru_lam[l, 0], False)
        hb = rg_lru_dir(ua, w_rg[l, 1], b_rg[l, 1], w_ig[l, 1], b_ig[l, 1], lru_lam[l, 1], True)
        ya = (hf + hb).astype(x.dtype) * jax.nn.silu(ga)

        yb = gqa_attention(q, k, v, q_norm_g[l], k_norm_g[l], tabs) * jax.nn.silu(gb)

        yc = bc * dwconv(cc * xc, conv_c_w[l], CONV_C_LEFT) * jax.nn.silu(gc)

        br = jnp.stack([ya, yb, yc], axis=2)
        pb = jnp.einsum('bskw,kwd->bskd', br, w_branch[l])
        gates = jax.nn.sigmoid(mg).reshape(B_, S, N_BRANCH, D)
        merged = jnp.einsum('bskd,bskd->bsd', gates, pb)
        x = x + gate[:, None, :] * (merged @ w_out[l])
    return x


_drawn_inputs = setup_inputs


def setup_inputs(seed=0):
    import zlib

    import numpy as np

    out = dict(_drawn_inputs(seed))
    spreads = {}
    factors = {'conv_a_b': 3.445, 'b_rg': 51.629, 'b_ig': 8.0, 'q_norm_g': 8.0, 'k_norm_g': 8.0}
    for name, (base, spread) in spreads.items():
        noise = np.random.default_rng([zlib.crc32(name.encode()), seed]).standard_normal(out[name].shape)
        drawn = base * np.exp(spread * noise) if base else spread * noise
        out[name] = __import__('jax').numpy.asarray(drawn.astype(out[name].dtype))
    for name, factor in factors.items():
        out[name] = (out[name] * factor).astype(out[name].dtype)
    return out
```

```python
from contextlib import ExitStack

import numpy as np

import concourse.bass as bass
from concourse import mybir

F32 = mybir.dt.float32
F32R = mybir.dt.float32r
ALU = mybir.AluOpType
ACT = mybir.ActivationFunctionType
AX_X = mybir.AxisListType.X

D = 1024
SEQ = 256
DEPTH = 2
P = 128
CT = D // P
PAIRS = CT // 2
ST = SEQ // P
N_HEADS, N_KV, HD = 8, 2, 128
RNN_BLOCKS, RNN_BW = 4, 256
CONV_A_W, CONV_A_LEFT = 4, 2
CONV_C_W, CONV_C_LEFT = 3, 1
N_BRANCH = 3
EPS = 1e-6
LRU_C = 8.0
GRID_W = 64
ROPE_THETA = 10000.0
SCALE = float(HD) ** -0.5

SIZES = dict(xa=D, ga=D, q=D, k=N_KV * HD, v=N_KV * HD, gb=D, xc=D, bc=D, cc=D, gc=D, mg=N_BRANCH * D)
COLUMN = {}
for _name in SIZES:
    COLUMN[_name] = sum(SIZES[m] for m in list(SIZES)[:list(SIZES).index(_name)])
N_IN = sum(SIZES.values())

BR_A, BR_B, BR_C = 0, 1, 2
UNITS = ([("xa", 0), ("xa", 1), ("q", 0), ("q", 1), ("kv", 0), ("rg", 0)]
         + [(n, 0) for n in ("xc", "cc", "bc", "gc")] + [("rg", 1)]
         + [(n, 1) for n in ("xc", "cc", "bc", "gc")]
         + [("mg", 2 * BR_C), ("mg", 2 * BR_C + 1), ("br", 2 * BR_C), ("br", 2 * BR_C + 1), ("ga", 0), ("ga", 1)]
         + [("mg", 2 * BR_A), ("mg", 2 * BR_A + 1), ("br", 2 * BR_A), ("br", 2 * BR_A + 1), ("gb", 0), ("gb", 1)]
         + [("mg", 2 * BR_B), ("mg", 2 * BR_B + 1), ("br", 2 * BR_B), ("br", 2 * BR_B + 1), ("out", 0), ("out", 1)])
NU = len(UNITS)
NT = 4 * NU
U = {name: i for i, name in enumerate(UNITS)}
U_OUT = U["out", 0]
LOADS = ([("unit", 0)] + [("ada", a) for a in range(4)] + [("unit", u) for u in range(1, U_OUT)]
         + [("ada", 4), ("ada", 5), ("unit", U_OUT), ("unit", U_OUT + 1)])
RAW_SLOTS = 3
assert len(LOADS) % RAW_SLOTS == 0
POS = {what: i for i, what in enumerate(LOADS)}
NADA = 6


def load_dmas(what):
    return 2 if what[0] == "unit" and UNITS[what[1]][0] == "rg" else 1


RAW_COUNT = [0] * RAW_SLOTS
RAW_READY = {}
for _pos, _what in enumerate(LOADS):
    RAW_COUNT[_pos % RAW_SLOTS] += 16 * load_dmas(_what)
    RAW_READY[_what] = RAW_COUNT[_pos % RAW_SLOTS]

BANKS = 4
BANK = {}
BANK_USES = [0] * BANKS
_b = 0
for _u, (_name, _) in enumerate(UNITS):
    for _i in range(8 if _name == "rg" else 2):
        BANK[_u, _i] = (_b % BANKS, BANK_USES[_b % BANKS])
        BANK_USES[_b % BANKS] += 1
        _b += 1

PARAMS = dict(norm_g=8, b_ada=24, conv_a_w=32, conv_a_b=8, b_rg=16, b_ig=16, lru_lam=16, conv_c_w=24,
              q_norm_g=1, k_norm_g=1, c=8)
COL = {}
for _name in PARAMS:
    COL[_name] = sum(PARAMS[m] for m in list(PARAMS)[:list(PARAMS).index(_name)])
ROWS_A = COL["lru_lam"]
N_ROWS = sum(PARAMS.values())
ROWS_B = N_ROWS - ROWS_A
COL["pos8"] = N_ROWS
COL["neg8"] = N_ROWS + 16
COL["neg16"] = N_ROWS + 32
N_COLS = N_ROWS + 48

C_ID, C_ROT, C_ONE, C_COS, C_SIN = 0, P, 2 * P, 3 * P, 3 * P + 2 * SEQ
N_CONST = 3 * P + 4 * SEQ

MERGED_AT = (122, 124, 126, 127)

V_STEPS = 121
S_STEPS = 78


def trunk_program(nc, x, c, w_ada, b_ada, norm_g, w_in, conv_a_w, conv_a_b, w_rg, b_rg, w_ig, b_ig,
                  lru_lam, q_norm_g, k_norm_g, conv_c_w, w_branch, w_out, consts, out):
    w_in_v = w_in.rearrange("l (t p) n -> l p t n", p=P)
    w_ada_v = w_ada.rearrange("l (t p) n -> l p t n", p=P)
    w_br_v = w_branch.rearrange("l b (t p) n -> l b p t n", p=P)
    w_out_v = w_out.rearrange("l (t p) n -> l p t n", p=P)
    w_rg_v = w_rg.rearrange("l d n (t p) m -> l d p (n t) m", p=P)
    w_ig_v = w_ig.rearrange("l d n (t p) m -> l d p (n t) m", p=P)

    with ExitStack() as ctx:
        def sb(name, shape, dt=F32):
            return ctx.enter_context(nc.sbuf_tensor(name, shape, dt))

        def psum(name, shape):
            return ctx.enter_context(nc.psum_tensor(name, shape, F32))

        gain = {}

        def sem(name, per_layer=0, ahead=False):
            s = ctx.enter_context(nc.semaphore(name))
            gain[id(s)] = (per_layer, per_layer if ahead else 0)
            return s

        def at(s, l, n):
            per_layer, start = gain[id(s)]
            return l * per_layer + (start + n)

        raw = sb("raw", [P, RAW_SLOTS, 8 * 512])
        w_hi = sb("w_hi", [P, 4, 8 * P], F32R)
        w_lo = sb("w_lo", [P, 4, 8 * P], F32R)
        xT = sb("xT", [P, CT, SEQ])
        h_hi = sb("h_hi", [P, CT, SEQ], F32R)
        h_lo = sb("h_lo", [P, CT, SEQ], F32R)
        y_hi = sb("y_hi", [P, CT, SEQ], F32R)
        y_lo = sb("y_lo", [P, CT, SEQ], F32R)
        padded = sb("padded", [P, CT, SEQ + 4])
        ua = sb("ua", [P, CT, SEQ])
        qkv = sb("qkv", [P, 12, SEQ])
        buf_i = sb("buf_i", [P, CT, SEQ])
        buf_r = sb("buf_r", [P, CT, SEQ])
        buf_t = sb("buf_t", [P, CT, SEQ])
        ya = sb("ya", [P, CT, SEQ])
        xc = sb("xc", [P, 4, SEQ])
        tmp = sb("tmp", [P, 4, SEQ])
        probs = sb("probs", [P, 4, SEQ])
        probsT = sb("probsT", [P, ST, 2 * SEQ])
        vtok = sb("vtok", [P, ST, N_KV, HD])
        cst = sb("cst", [P, N_CONST])
        par = sb("par", [P, DEPTH, N_COLS])
        cur = sb("cur", [P, N_COLS])
        rstd = sb("rstd", [P, SEQ])
        eps_t = sb("eps_t", [P, 1])
        eps_col = eps_t[:, 0:1]
        mods = sb("mods", [P, 4, CT])
        stat = sb("stat", [P, 4, 4])

        def yc(ch, n=1):
            if ch < 4:
                return padded[:, 4 + ch:4 + ch + n, CONV_A_LEFT:CONV_A_LEFT + SEQ]
            return ua[:, ch:ch + n, :]

        def whole(buffer):
            return lambda ch, n: buffer[:, ch:ch + n, :]

        yb = buf_t
        merged = buf_r
        gates = buf_i
        small = tmp[:, 0, 0:8 * 32].rearrange("p (a b) -> p a b", a=8)

        ident = cst[:, C_ID:C_ID + P]
        rot = cst[:, C_ROT:C_ROT + P]
        ones = cst[:, C_ONE:C_ONE + P]
        cos2 = cst[:, C_COS:C_COS + 2 * SEQ]
        sin2 = cst[:, C_SIN:C_SIN + 2 * SEQ]

        stream = psum("stream", [P, BANKS, 512])
        scores = psum("scores", [P, 4, SEQ])
        turned = psum("turned", [P, 2, 512])
        sums = [scores[:, 0:2, :].rearrange("p a b -> p (a b)"), scores[:, 2:4, :].rearrange("p a b -> p (a b)")]
        mod_ps = scores[:, 2, :]

        raw_loaded = [sem(f"raw_loaded{i}", RAW_COUNT[i]) for i in range(RAW_SLOTS)]
        whi_ready = sem("whi_ready", NT)
        wlo_ready = sem("wlo_ready", NT, ahead=True)
        tile_done = sem("tile_done", NT, ahead=True)
        bank_free = [sem(f"bank_free{b}", BANK_USES[b], ahead=True) for b in range(BANKS)]
        ada_done = sem("ada_done", NADA, ahead=True)
        x_squared = sem("x_squared", PAIRS)
        x_summed = sem("x_summed", 1)
        x_rstd = sem("x_rstd", 1)
        cur_ready = sem("cur_ready", 1)
        x_normed = sem("x_normed", CT)
        mods_ready = sem("mods_ready", 1)
        hhi_ready = sem("hhi_ready", CT)
        h_ready = sem("h_ready", CT)
        ua_ready = sem("ua_ready", PAIRS)
        yhi_ready = sem("yhi_ready", 5 * PAIRS)
        y_ready = sem("y_ready", 5 * PAIRS)
        q_squared = sem("q_squared", 5)
        q_summed = sem("q_summed", 5)
        q_rstd = sem("q_rstd", 5)
        q_normed = sem("q_normed", 5)
        q_rotated = sem("q_rotated", 5)
        q_ready = sem("q_ready", 5)
        v_turned = sem("v_turned", 1)
        v_ready = sem("v_ready", 1)
        rg_exp = sem("rg_exp", 4)
        rg_w = sem("rg_w", 4)
        rg_root = sem("rg_root", 4)
        scanned = sem("scanned", 4)
        sigmoids = sem("sigmoids", 12)
        gated = sem("gated", 12)
        merged_ready = sem("merged_ready", PAIRS)
        scored = sem("scored", 4)
        max_ready = sem("max_ready", 4)
        exp_done = sem("exp_done", 4)
        probs_ready = sem("probs_ready", 4)
        probs_turned = sem("probs_turned", 4)
        probsT_ready = sem("probsT_ready", 8)
        o_summed = sem("o_summed", 4)
        o_ready = sem("o_ready", 4)
        gate_ready = sem("gate_ready", 1)
        v_step = sem("v_step", V_STEPS)
        s_step = sem("s_step", S_STEPS)
        loaded = sem("loaded")
        x_loaded = sem("x_loaded")
        par_turned = sem("par_turned")
        par_copied = sem("par_copied")
        lam_exp = sem("lam_exp")
        v_first = sem("v_first")
        x_turned = sem("x_turned")
        x_ready = sem("x_ready")
        out_turned = sem("out_turned")
        out_ready = sem("out_ready")
        stored = sem("stored")

        xtok = buf_i[:, :, :].rearrange("p t n -> p (t n)").rearrange("p (s n) -> p s n", s=ST)
        rows = xc[:, :, 0:P]

        class Steps:

            def __init__(self, step, l):
                self.step, self.l, self.n = step, l, 0

            def next(self):
                self.n += 1
                return 1

            def now(self, back=0):
                return at(self.step, self.l, self.n - back)

        def raw_tile(n):
            u, t = divmod(n, 4)
            slot = POS["unit", u] % RAW_SLOTS
            if UNITS[u][0] == "rg":
                return raw[:, slot, 1024 * t:1024 * (t + 1)].rearrange("p (k m) -> p k m", k=8)
            return raw[:, slot, :].rearrange("p (k m) -> p k m", k=8)[:, :, P * t:P * (t + 1)]

        def pair_ps(u, i):
            return stream[:, BANK[u, i][0], :].rearrange("p (a b) -> p a b", a=2)

        def bank(u, i):
            return BANK[u, i][0]

        def freed_at(l, u, i, layers_back=0):
            b, use = BANK[u, i]
            return at(bank_free[b], l, use + 1 - layers_back * BANK_USES[b])

        block = ctx.enter_context(nc.Block())

        @block.sync
        def _(sync):
            with sync.Fori(0, DEPTH) as l:
                for pos, (kind, i) in enumerate(LOADS):
                    slot = pos % RAW_SLOTS
                    before = pos - RAW_SLOTS
                    user, ui = LOADS[before % len(LOADS)]
                    back = 1 if before < 0 else 0
                    if user == "unit":
                        sync.wait_ge(wlo_ready, at(wlo_ready, l, 4 * ui + 4 - back * NT))
                    else:
                        sync.wait_ge(ada_done, at(ada_done, l, ui + 1 - back * NADA))
                    dst = raw[:, slot, :].rearrange("p (k m) -> p k m", k=8)
                    if kind == "ada":
                        src = w_ada_v[l, :, :, 512 * i:512 * i + 512]
                    else:
                        name, part = UNITS[i]
                        if name == "rg":
                            for kind_i, w in enumerate((w_rg_v, w_ig_v)):
                                d = raw[:, slot, 2048 * kind_i:2048 * (kind_i + 1)].rearrange("p (k m) -> p k m", k=8)
                                sync.dma_start(d, w[l, part]).then_inc(raw_loaded[slot], 16)
                            continue
                        if name == "br":
                            branch, half = divmod(part, 2)
                            src = w_br_v[l, branch, :, :, 512 * half:512 * half + 512]
                        elif name == "out":
                            src = w_out_v[l, :, :, 512 * part:512 * part + 512]
                        else:
                            col = COLUMN["k" if name == "kv" else name] + 512 * part
                            src = w_in_v[l, :, :, col:col + 512]
                    sync.dma_start(dst, src).then_inc(raw_loaded[slot], 16)
            sync.wait_ge(out_ready, 4)
            sync.dma_start(out[0].rearrange("(s p) n -> p s n", p=P), xtok).then_inc(stored, 16)
            sync.wait_ge(stored, 16)

        @block.scalar
        def _(act):
            act.dma_start(cst[:], consts).then_inc(loaded, 16)
            n_loads = 1

            def load_rows(group, at, src, n):
                act.dma_start(rows[at:at + n, group, :], src).then_inc(loaded, 16)

            for l in range(DEPTH):
                for name, src in (("norm_g", norm_g[l]), ("b_ada", b_ada[l]),
                                  ("conv_a_w", conv_a_w[l].rearrange("a b -> (a b)")), ("conv_a_b", conv_a_b[l]),
                                  ("b_rg", b_rg[l].rearrange("a b -> (a b)")), ("b_ig", b_ig[l].rearrange("a b -> (a b)")),
                                  ("lru_lam", lru_lam[l].rearrange("a b -> (a b)")),
                                  ("conv_c_w", conv_c_w[l].rearrange("a b -> (a b)")),
                                  ("q_norm_g", q_norm_g[l]), ("k_norm_g", k_norm_g[l]), ("c", c[0])):
                    second = COL[name] >= ROWS_A
                    load_rows(2 * l + second, COL[name] - (ROWS_A if second else 0),
                              src.rearrange("(a b) -> a b", b=P), PARAMS[name])
                    n_loads += 1
            act.dma_start(xtok, x[0].rearrange("(s p) n -> p s n", p=P)).then_inc(x_loaded, 16)
            assert n_loads == 1 + 11 * DEPTH

            lam = par[:, :, COL["lru_lam"]:COL["lru_lam"] + 16]
            e_l = small[:, 0, :].rearrange("p (a b) -> p a b", a=DEPTH)
            act.wait_ge(par_copied, 1)
            act.activation(e_l, lam, ACT.Abs).then_inc(lam_exp, 1)
            act.wait_ge(lam_exp, 1)
            act.activation(e_l, e_l, ACT.Exp, scale=-1.0).then_inc(lam_exp, 1)
            act.wait_ge(x_ready, PAIRS)

            with act.Fori(0, DEPTH) as l:
                own = Steps(s_step, l)

                def split_hi(n):
                    u, t = divmod(n, 4)
                    if t == 0:
                        slot = POS["unit", u] % RAW_SLOTS
                        act.wait_ge(raw_loaded[slot], at(raw_loaded[slot], l, RAW_READY["unit", u]))
                    act.wait_ge(tile_done, at(tile_done, l, n - 3))
                    act.activation(w_hi[:, t, :].rearrange("p (k m) -> p k m", k=8), raw_tile(n),
                                   ACT.Copy).then_inc(whi_ready, 1)

                def split_y(i, pair, src, dst):
                    act.activation(dst[:, 2 * pair:2 * pair + 2, :], src(2 * pair, 2),
                                   ACT.Copy).then_inc(yhi_ready, 1)

                def squares(i):
                    u, pair = U["q", 0] + i // 2, i % 2
                    ps = pair_ps(u, pair)
                    if i >= 2 and i < 5:
                        act.wait_ge(q_summed, at(q_summed, l, i - 1))
                    if i < 5:
                        act.activation(tmp[:, 2 * (i % 2):2 * (i % 2) + 2, :], ps, ACT.Square).then_inc(q_squared, 1)
                    act.activation(qkv[:, 2 * i:2 * i + 2, :], ps, ACT.Copy).then_inc(bank_free[bank(u, pair)], 1)

                def q_norm(i):
                    act.wait_ge(q_summed, at(q_summed, l, i + 1))
                    if i >= 2:
                        act.wait_ge(q_normed, at(q_normed, l, i - 1))
                    r = probs[:, 2 * (i % 2):2 * (i % 2) + 2, :].rearrange("p a b -> p (a b)")
                    act.activation(r, sums[i % 2], ACT.Ln, bias=eps_col, scale=1.0 / HD).then_inc(s_step, own.next())
                    act.wait_ge(s_step, own.now())
                    act.activation(r, r, ACT.Exp, scale=-0.5).then_inc(q_rstd, 1)

                def rg_sigmoids(d, t):
                    u = U["rg", d]
                    kind, half = divmod(t, 2)
                    if d == 1 and t == 0:
                        act.wait_ge(scanned, at(scanned, l, 2))
                    dst, bias = (buf_r, "b_rg") if kind == 0 else (buf_i, "b_ig")
                    for j in range(4):
                        ch = 4 * half + j
                        col = COL[bias] + 8 * d + ch
                        ins = act.activation(dst[:, ch, :], pair_ps(u, 2 * t + j // 2)[:, j % 2, :],
                                             ACT.Sigmoid, bias=cur[:, col:col + 1])
                        if j % 2:
                            ins.then_inc(bank_free[bank(u, 2 * t + j // 2)], 1)
                        else:
                            ins.then_inc(s_step, own.next())

                def rg_scaled(d, half, dst, func, coef):
                    for j in range(4):
                        ch = 4 * half + j
                        col = COL[coef] + 8 * d + ch
                        ins = act.activation(dst(ch), buf_r[:, ch, :], func, scale=cur[:, col:col + 1])
                        if j < 3 or coef != "neg16":
                            ins.then_inc(s_step, own.next())
                        else:
                            ins.then_inc(rg_exp, 1)

                def rg_math(d, s):
                    if s in (0, 3):
                        half = s // 3
                        act.wait_ge(bank_free[bank(U["rg", d], 2 * half + 1)], freed_at(l, U["rg", d], 2 * half + 1))
                        rg_scaled(d, half, lambda ch: buf_t[:, ch, :], ACT.Tanh, "pos8")
                    elif s in (1, 4):
                        half = s // 3
                        if half == 1 or d == 1:
                            act.wait_ge(rg_w, at(rg_w, l, 2 * d + half))
                        rg_scaled(d, half, lambda ch: tmp[:, ch % 4, :], ACT.Exp, "neg16")
                    elif s in (2, 5):
                        rg_scaled(d, s // 3, lambda ch: buf_r[:, ch, :], ACT.Exp, "neg8")
                    else:
                        half = s - 6
                        act.wait_ge(rg_w, at(rg_w, l, 2 * d + half + 1))
                        t4 = buf_t[:, 4 * half:4 * half + 4, :]
                        act.activation(t4, t4, ACT.Sqrt).then_inc(rg_root, 1)

                def silu_sigmoid(i, u, pair):
                    slot = i % 2
                    if i >= 2:
                        act.wait_ge(gated, at(gated, l, i - 1))
                    act.activation(xc[:, 2 * slot:2 * slot + 2, :], pair_ps(u, pair),
                                   ACT.Sigmoid).then_inc(sigmoids, 1)

                def softmax_exp(g):
                    act.wait_ge(max_ready, at(max_ready, l, g + 1))
                    if g:
                        act.wait_ge(probs_turned, at(probs_turned, l, g))
                    for j in range(4):
                        ins = act.activation(probs[:, j, :], scores[:, j, :], ACT.Exp, bias=stat[:, 1, j:j + 1],
                                             scale=SCALE, accum_out=stat[:, 2, j:j + 1])
                        if j < 3:
                            ins.then_inc(s_step, own.next())
                    ins.then_inc(exp_done, 1)

                def probs_out(g):
                    act.wait_ge(probs_turned, at(probs_turned, l, g + 1))
                    if g:
                        act.wait_ge(o_summed, at(o_summed, l, g))
                    for s in range(ST):
                        act.activation(probsT[:, s, :], turned[:, s, :], ACT.Copy).then_inc(probsT_ready, 1)

                def consume(u, pair):
                    name, part = UNITS[u]
                    act.wait_ge(tile_done, at(tile_done, l, 4 * u + 2 * pair + 2))
                    ps = pair_ps(u, pair)
                    if name == "xa":
                        ch = 4 * part + 2 * pair
                        act.activation(padded[:, ch:ch + 2, CONV_A_LEFT:CONV_A_LEFT + SEQ], ps, ACT.Copy).then_inc(bank_free[bank(u, pair)], 1)
                    elif name in ("q", "kv"):
                        i = 2 * (u - U["q", 0]) + pair
                        squares(i)
                    elif name == "xc":
                        if part == 1:
                            act.wait_ge(gated, at(gated, l, pair + 1))
                        act.activation(xc[:, 2 * pair:2 * pair + 2, :], ps, ACT.Copy).then_inc(bank_free[bank(u, pair)], 1)
                    elif name == "gc":
                        act.wait_ge(bank_free[bank(U["cc", part], pair)], freed_at(l, U["cc", part], pair))
                        act.activation(xc[:, 2 * pair:2 * pair + 2, :], ps, ACT.Sigmoid).then_inc(sigmoids, 1)
                    elif name in ("ga", "gb"):
                        silu_sigmoid((4 if name == "ga" else 8) + 2 * part + pair, u, pair)
                    elif name == "mg":
                        ch = 4 * (part % 2) + 2 * pair
                        act.activation(gates[:, ch:ch + 2, :], ps, ACT.Sigmoid).then_inc(bank_free[bank(u, pair)], 1)

                for pair in range(PAIRS):
                    act.wait_ge(bank_free[bank(U_OUT + pair // 2, pair % 2)], freed_at(l, U_OUT + pair // 2, pair % 2, layers_back=1))
                    act.activation(buf_i[:, 2 * pair:2 * pair + 2, :], xT[:, 2 * pair:2 * pair + 2, :],
                                   ACT.Square).then_inc(x_squared, 1)
                split_hi(0)
                act.wait_ge(x_summed, at(x_summed, l, 1))
                act.activation(rstd[:], scores[:, 0, :], ACT.Ln, bias=eps_col, scale=1.0 / D).then_inc(s_step, own.next())
                act.wait_ge(s_step, own.now())
                act.activation(rstd[:], rstd[:], ACT.Exp, scale=-0.5).then_inc(x_rstd, 1)
                for n in range(1, 4):
                    split_hi(n)
                act.wait_ge(mods_ready, at(mods_ready, l, 1))
                for k in range(CT):
                    act.activation(h_hi[:, k, :], buf_r[:, k, :], ACT.Identity, bias=mods[:, 0, k:k + 1],
                                   scale=mods[:, 2, k:k + 1]).then_inc(hhi_ready, 1)

                for n in range(4, NT):
                    u, t = divmod(n, 4)
                    split_hi(n)
                    if UNITS[u - 1][0] == "rg":
                        act.wait_ge(tile_done, at(tile_done, l, 4 * (u - 1) + t + 1))
                        rg_sigmoids(UNITS[u - 1][1], t)
                    elif t % 2:
                        consume(u - 1, t // 2)
                    if n in (6, 8, 10, 12):
                        i = (n - 6) // 2
                        act.wait_ge(ua_ready, at(ua_ready, l, i + 1))
                        split_y(0, i, whole(ua), y_hi)
                    if n in (16, 18, 20, 22, 23):
                        q_norm(min((n - 16) // 2 + (n == 23), 4))
                    if 28 <= n < 36:
                        rg_math(0, n - 28)
                    if 48 <= n < 56:
                        rg_math(1, n - 48)
                    if n in (64, 65, 66, 67):
                        act.wait_ge(gated, at(gated, l, n - 63))
                        split_y(1, n - 64, yc, y_hi)
                    if n in (72, 80, 88, 96):
                        softmax_exp((n - 72) // 8)
                    if n in (76, 84, 92, 100):
                        probs_out((n - 76) // 8)
                    if n in (82, 84, 86, 88):
                        i = (n - 82) // 2
                        act.wait_ge(gated, at(gated, l, 5 + i))
                        split_y(2, i, whole(ya), y_hi)
                    if n in (106, 108, 110, 112):
                        i = (n - 106) // 2
                        act.wait_ge(gated, at(gated, l, 9 + i))
                        split_y(3, i, whole(yb), y_hi)
                    if n in MERGED_AT:
                        i = MERGED_AT.index(n)
                        act.wait_ge(merged_ready, at(merged_ready, l, i + 1))
                        split_y(4, i, whole(merged), h_hi)
                assert own.n == S_STEPS, own.n

        @block.vector
        def _(vec):
            vec.memset(padded[:, :, :], 0.0).then_inc(v_first, 1)
            vec.memset(eps_col, EPS).then_inc(v_first, 1)
            vec.sem_inc(wlo_ready, NT)
            for b in range(BANKS):
                vec.sem_inc(bank_free[b], BANK_USES[b])
            vec.wait_ge(par_turned, DEPTH)
            vec.tensor_copy(par[:, :, 0:N_ROWS], scores[:, 0:4:2, 0:N_ROWS]).then_inc(par_copied, 1)
            lam = par[:, :, COL["lru_lam"]:COL["lru_lam"] + 16]

            def scratch(i):
                return small[:, i, :].rearrange("p (a b) -> p a b", a=DEPTH)

            e_l, s_l, s2, q_l, sp = (scratch(i) for i in range(5))
            done = [2]

            def chain(instruction):
                instruction.then_inc(v_first, 1)
                done[0] += 1
                vec.wait_ge(v_first, done[0])

            vec.wait_ge(lam_exp, 2)
            chain(vec.tensor_scalar(s_l, e_l, 2.0, None, ALU.add))
            chain(vec.reciprocal(s_l, s_l))
            chain(vec.tensor_tensor(s_l, s_l, e_l, ALU.mult))
            chain(vec.tensor_tensor(s2, s_l, s_l, ALU.mult))
            chain(vec.tensor_scalar(q_l, s2, 1.0 / 15, None, ALU.mult))
            for odd in (13, 11, 9, 7, 5, 3):
                chain(vec.scalar_tensor_tensor(out=q_l, in0=q_l, scalar=1.0 / odd, in1=s2, op0=ALU.add, op1=ALU.mult))
            chain(vec.scalar_tensor_tensor(out=q_l, in0=q_l, scalar=1.0, in1=s_l, op0=ALU.add, op1=ALU.mult))
            chain(vec.tensor_scalar(sp, lam, -1.0, 0.0, ALU.mult, ALU.max))
            chain(vec.scalar_tensor_tensor(out=sp, in0=q_l, scalar=2.0, in1=sp, op0=ALU.mult, op1=ALU.add))
            for name, factor in (("pos8", LRU_C), ("neg8", -LRU_C), ("neg16", -2 * LRU_C)):
                chain(vec.tensor_scalar(par[:, :, COL[name]:COL[name] + 16], sp, factor, None, ALU.mult))
            for pair in range(PAIRS):
                vec.wait_ge(x_turned, pair + 1)
                vec.tensor_copy(xT[:, 2 * pair:2 * pair + 2, :],
                                stream[:, pair, :].rearrange("p (a b) -> p a b", a=2)).then_inc(x_ready, 1)

            with vec.Fori(0, DEPTH) as l:
                own = Steps(v_step, l)

                def split_lo(n):
                    t = n % 4
                    vec.wait_ge(whi_ready, at(whi_ready, l, n + 1))
                    vec.tensor_tensor(w_lo[:, t, :].rearrange("p (k m) -> p k m", k=8), raw_tile(n),
                                      w_hi[:, t, :].bitcast(F32).rearrange("p (k m) -> p k m", k=8),
                                      ALU.subtract).then_inc(wlo_ready, 1)

                def split_y(i, pair, src, hi, lo):
                    vec.wait_ge(yhi_ready, at(yhi_ready, l, PAIRS * i + pair + 1))
                    s = slice(2 * pair, 2 * pair + 2)
                    vec.tensor_tensor(lo[:, s, :], src(2 * pair, 2), hi[:, s, :].bitcast(F32),
                                      ALU.subtract).then_inc(y_ready, 1)

                def conv(pair, src, shift0, taps, weight, bias, dst, src_tile, signal=None):
                    chs = (2 * pair, 2 * pair + 1)
                    for k in range(taps):
                        for i, ch in enumerate(chs):
                            win = src[:, src_tile + i, shift0 + k:shift0 + k + SEQ]
                            col = COL[weight] + 8 * k + ch
                            wk = cur[:, col:col + 1]
                            if k == 0:
                                b = cur[:, COL[bias] + ch:COL[bias] + ch + 1] if bias else None
                                ins = vec.tensor_scalar(dst(ch, 1)[:, 0, :], win, wk, b, ALU.mult,
                                                        ALU.add if bias else ALU.bypass)
                            else:
                                vec.wait_ge(v_step, own.now(back=1))
                                ins = vec.scalar_tensor_tensor(out=dst(ch, 1)[:, 0, :], in0=win, scalar=wk,
                                                               in1=dst(ch, 1)[:, 0, :], op0=ALU.mult, op1=ALU.add)
                            if signal is not None and k == taps - 1 and i == 1:
                                ins.then_inc(signal, 1)
                            else:
                                ins.then_inc(v_step, own.next())

                def q_norm(i):
                    vec.wait_ge(q_rstd, at(q_rstd, l, i + 1))
                    g = COL["q_norm_g" if i < 4 else "k_norm_g"]
                    z = qkv[:, 2 * i:2 * i + 2, :]
                    vec.scalar_tensor_tensor(out=z, in0=z, scalar=cur[:, g:g + 1],
                                             in1=probs[:, 2 * (i % 2):2 * (i % 2) + 2, :], op0=ALU.mult,
                                             op1=ALU.mult).then_inc(q_normed, 1)

                def rope(i):
                    vec.wait_ge(q_rotated, at(q_rotated, l, i + 1))
                    z = qkv[:, 2 * i:2 * i + 2, :].rearrange("p a b -> p (a b)")
                    r = probsT[:, i % 2, :]
                    vec.tensor_tensor(r, turned[:, i % 2, :], sin2, ALU.mult).then_inc(v_step, own.next())
                    vec.tensor_tensor(z, z, cos2, ALU.mult).then_inc(v_step, own.next())
                    vec.wait_ge(v_step, own.now())
                    vec.tensor_tensor(z, z, r, ALU.add).then_inc(q_ready, 1)

                def rg_math(d, s):
                    if s in (0, 3):
                        half = s // 3
                        vec.wait_ge(bank_free[bank(U["rg", d], 4 + 2 * half + 1)], freed_at(l, U["rg", d], 4 + 2 * half + 1))
                        z = buf_i[:, 4 * half:4 * half + 4, :]
                        vec.tensor_tensor(z, z, ua_of(half), ALU.mult).then_inc(v_step, own.next())
                    if s in (2, 5):
                        half = (s - 2) // 3
                        vec.wait_ge(rg_exp, at(rg_exp, l, 2 * d + half + 1))
                        t4 = buf_t[:, 4 * half:4 * half + 4, :]
                        vec.scalar_tensor_tensor(out=t4.rearrange("p a b -> p (a b)"),
                                                 in0=tmp[:, :, :].rearrange("p a b -> p (a b)"), scalar=1.0,
                                                 in1=t4.rearrange("p a b -> p (a b)"), op0=ALU.add,
                                                 op1=ALU.mult).then_inc(rg_w, 1)
                    if s in (9, 10):
                        half = s - 9
                        vec.wait_ge(rg_root, at(rg_root, l, 2 * d + half + 1))
                        z = buf_i[:, 4 * half:4 * half + 4, :]
                        vec.tensor_tensor(z, z, buf_t[:, 4 * half:4 * half + 4, :], ALU.mult).then_inc(v_step, own.next())
                    if s in (11, 12):
                        half = s - 11
                        vec.wait_ge(v_step, own.now())
                        for j in range(4):
                            ch = 4 * half + j
                            a, u_, o = buf_r[:, ch, :], buf_i[:, ch, :], (ya if d == 0 else buf_t)[:, ch, :]
                            if d == 1:
                                a, u_, o = a[:, ::-1], u_[:, ::-1], o[:, ::-1]
                            ins = vec.tensor_tensor_scan(o, a, u_, 0.0, ALU.mult, ALU.add)
                            if j < 3:
                                ins.then_inc(v_step, own.next())
                            else:
                                ins.then_inc(scanned, 1)
                    if d == 1 and s in (13, 14):
                        half = s - 13
                        vec.wait_ge(scanned, at(scanned, l, 3 + half))
                        z = ya[:, 4 * half:4 * half + 4, :]
                        vec.tensor_tensor(z, z, buf_t[:, 4 * half:4 * half + 4, :], ALU.add).then_inc(v_step, own.next())

                def ua_of(half):
                    return ua[:, 4 * half:4 * half + 4, :]

                def silu_gate(i, u, pair, y, ch):
                    vec.wait_ge(sigmoids, at(sigmoids, l, i + 1))
                    z = xc[:, 2 * (i % 2):2 * (i % 2) + 2, :]
                    vec.tensor_tensor(z, z, pair_ps(u, pair), ALU.mult).then_inc(bank_free[bank(u, pair)], 1)
                    vec.wait_ge(bank_free[bank(u, pair)], freed_at(l, u, pair))
                    vec.tensor_tensor(y(ch, 2), y(ch, 2), z, ALU.mult).then_inc(gated, 1)

                def softmax_max(g):
                    vec.wait_ge(scored, at(scored, l, g + 1))
                    vec.tensor_reduce(stat[:, 0, :], scores[:, :, :], AX_X, ALU.max).then_inc(v_step, own.next())
                    vec.wait_ge(v_step, own.now())
                    vec.tensor_scalar(stat[:, 1, :], stat[:, 0, :], -SCALE, None, ALU.mult).then_inc(max_ready, 1)

                def softmax_norm(g):
                    vec.wait_ge(exp_done, at(exp_done, l, g + 1))
                    vec.reciprocal(stat[:, 3, :], stat[:, 2, :]).then_inc(v_step, own.next())
                    vec.wait_ge(v_step, own.now())
                    for j in range(4):
                        ins = vec.tensor_scalar(probs[:, j, :], probs[:, j, :], stat[:, 3, j:j + 1], None, ALU.mult)
                        if j < 3:
                            ins.then_inc(v_step, own.next())
                    ins.then_inc(probs_ready, 1)

                def consume(u, pair):
                    name, part = UNITS[u]
                    ps = pair_ps(u, pair)
                    if name == "xa":
                        vec.wait_ge(bank_free[bank(u, pair)], freed_at(l, u, pair))
                        ch = 4 * part + 2 * pair
                        conv(ch // 2, padded, 0, CONV_A_W, "conv_a_w", "conv_a_b", whole(ua), ch, signal=ua_ready)
                    elif name == "cc":
                        vec.wait_ge(tile_done, at(tile_done, l, 4 * u + 2 * pair + 2))
                        vec.wait_ge(bank_free[bank(U["xc", part], pair)], freed_at(l, U["xc", part], pair))
                        vec.tensor_tensor(padded[:, 2 * pair:2 * pair + 2, CONV_A_LEFT:CONV_A_LEFT + SEQ], ps,
                                                xc[:, 2 * pair:2 * pair + 2, :], ALU.mult).then_inc(bank_free[bank(u, pair)], 1)
                    elif name == "bc":
                        vec.wait_ge(tile_done, at(tile_done, l, 4 * u + 2 * pair + 2))
                        vec.wait_ge(v_step, own.now())
                        ch = 4 * part + 2 * pair
                        vec.tensor_tensor(yc(ch, 2), yc(ch, 2), ps, ALU.mult).then_inc(bank_free[bank(u, pair)], 1)
                    elif name == "gc":
                        silu_gate(2 * part + pair, u, pair, yc, 4 * part + 2 * pair)
                    elif name == "ga":
                        silu_gate(4 + 2 * part + pair, u, pair, whole(ya), 4 * part + 2 * pair)
                    elif name == "gb":
                        silu_gate(8 + 2 * part + pair, u, pair, whole(yb), 4 * part + 2 * pair)
                    elif name == "br":
                        branch, half = divmod(part, 2)
                        ch = 4 * half + 2 * pair
                        vec.wait_ge(tile_done, at(tile_done, l, 4 * u + 2 * pair + 2))
                        vec.wait_ge(bank_free[bank(U["mg", part], pair)], freed_at(l, U["mg", part], pair))
                        m, g = merged[:, ch:ch + 2, :], gates[:, ch:ch + 2, :]
                        if branch == BR_C:
                            vec.tensor_tensor(m, g, ps, ALU.mult).then_inc(bank_free[bank(u, pair)], 1)
                        else:
                            z = tmp[:, 2 * pair:2 * pair + 2, :]
                            vec.tensor_tensor(z, g, ps, ALU.mult).then_inc(bank_free[bank(u, pair)], 1)
                            vec.wait_ge(bank_free[bank(u, pair)], freed_at(l, u, pair))
                            ins = vec.tensor_tensor(m, m, z, ALU.add)
                            if branch == BR_B:
                                ins.then_inc(merged_ready, 1)
                            else:
                                ins.then_inc(v_step, own.next())
                    elif name == "out":
                        vec.wait_ge(tile_done, at(tile_done, l, 4 * u + 2 * pair + 2))
                        vec.wait_ge(gate_ready, at(gate_ready, l, 1))
                        for i in range(2):
                            ch = 4 * part + 2 * pair + i
                            ins = vec.scalar_tensor_tensor(out=xT[:, ch, :], in0=ps[:, i, :],
                                                           scalar=mods[:, 3, ch:ch + 1], in1=xT[:, ch, :],
                                                           op0=ALU.mult, op1=ALU.add)
                            if i == 0:
                                ins.then_inc(v_step, own.next())
                        ins.then_inc(bank_free[bank(u, pair)], 1)

                vec.tensor_copy(cur[:], par[:, bass.ds(l, 1), :].rearrange("p a b -> p (a b)")).then_inc(cur_ready, 1)
                for n in range(4):
                    split_lo(n)
                vec.wait_ge(x_rstd, at(x_rstd, l, 1))
                for k in range(CT):
                    vec.tensor_tensor(buf_r[:, k, :], xT[:, k, :], rstd[:], ALU.mult).then_inc(x_normed, 1)
                vec.wait_ge(ada_done, at(ada_done, l, 4))
                vec.wait_ge(cur_ready, at(cur_ready, l, 1))
                vec.tensor_tensor(mods[:, 0:2, :], mod_ps[:, 0:16].rearrange("p (a b) -> p a b", a=2),
                                          cur[:, COL["b_ada"]:COL["b_ada"] + 16].rearrange("p (a b) -> p a b", a=2),
                                          ALU.add).then_inc(v_step, own.next())
                vec.wait_ge(v_step, own.now())
                vec.scalar_tensor_tensor(out=mods[:, 2, :], in0=mods[:, 1, :], scalar=1.0,
                                         in1=cur[:, COL["norm_g"]:COL["norm_g"] + 8], op0=ALU.add,
                                         op1=ALU.mult).then_inc(mods_ready, 1)
                vec.wait_ge(mods_ready, at(mods_ready, l, 1))
                for k in range(CT):
                    vec.tensor_scalar(buf_t[:, k, :], buf_r[:, k, :], mods[:, 2, k:k + 1], mods[:, 0, k:k + 1],
                                              ALU.mult, ALU.add).then_inc(v_step, own.next())
                    vec.wait_ge(hhi_ready, at(hhi_ready, l, k + 1))
                    vec.wait_ge(v_step, own.now())
                    vec.tensor_tensor(h_lo[:, k, :], buf_t[:, k, :], h_hi[:, k, :].bitcast(F32),
                                      ALU.subtract).then_inc(h_ready, 1)

                for n in range(4, NT):
                    u, t = divmod(n, 4)
                    split_lo(n)
                    if UNITS[u - 1][0] != "rg" and t % 2:
                        consume(u - 1, t // 2)
                    if n in (6, 8, 10, 12):
                        split_y(0, (n - 6) // 2, whole(ua), y_hi, y_lo)
                    if n in (16, 18, 20, 22, 23):
                        q_norm(min((n - 16) // 2 + (n == 23), 4))
                    if n in (19, 21, 23, 25, 27):
                        rope((n - 19) // 2)
                    if n == 28:
                        vec.wait_ge(v_turned, at(v_turned, l, 1))
                        vec.tensor_copy(vtok[:, :, :, :].rearrange("p a b c -> p (a b c)"),
                                        turned[:, 1, :]).then_inc(v_ready, 1)
                    for d, start in ((0, 28), (1, 48)):
                        if start <= n < start + 15:
                            rg_math(d, n - start)
                    for part, start in ((0, 34), (1, 54)):
                        if n in (start, start + 2):
                            pair = (n - start) // 2
                            vec.wait_ge(bank_free[bank(U["cc", part], pair)], freed_at(l, U["cc", part], pair))
                            conv(2 * part + pair, padded, CONV_A_LEFT - CONV_C_LEFT, CONV_C_W, "conv_c_w", None,
                                 yc, 2 * pair)
                    if n in (64, 65, 66, 67):
                        split_y(1, n - 64, yc, y_hi, y_lo)
                    if n in (72, 80, 88, 96):
                        softmax_max((n - 72) // 8)
                    if n in (73, 81, 89, 97):
                        softmax_norm((n - 73) // 8)
                    if n in (80, 88, 96, 104):
                        g = (n - 80) // 8
                        vec.wait_ge(o_summed, at(o_summed, l, g + 1))
                        vec.tensor_copy(yb[:, 2 * g:2 * g + 2, :],
                                        turned[:, 0, :].rearrange("p (a b) -> p a b", a=2)).then_inc(o_ready, 1)
                    if n in (82, 84, 86, 88):
                        split_y(2, (n - 82) // 2, whole(ya), y_hi, y_lo)
                    if n in (106, 108, 110, 112):
                        split_y(3, (n - 106) // 2, whole(yb), y_hi, y_lo)
                    if n in MERGED_AT:
                        split_y(4, MERGED_AT.index(n), whole(merged), h_hi, h_lo)
                    if n == 128:
                        vec.wait_ge(ada_done, at(ada_done, l, NADA))
                        vec.tensor_tensor(mods[:, 3, :], mod_ps[:, 0:8], cur[:, COL["b_ada"] + 16:COL["b_ada"] + 24],
                                          ALU.add).then_inc(gate_ready, 1)
                for pair in range(2):
                    consume(NU - 1, pair)
                assert own.n == V_STEPS, own.n

            for i in range(4):
                vec.wait_ge(out_turned, i + 1)
                s, half = divmod(i, 2)
                vec.tensor_copy(xtok[:, s, 512 * half:512 * half + 512], stream[:, i, :]).then_inc(out_ready, 1)

        @block.tensor
        def _(pe):
            pe.sem_inc(tile_done, NT)
            pe.sem_inc(ada_done, NADA)
            pe.wait_ge(loaded, 16 * (1 + 11 * DEPTH))
            for l in range(DEPTH):
                pe.transpose(scores[:, 2 * l, 0:ROWS_A], rows[0:ROWS_A, 2 * l, :], ident[0:ROWS_A, 0:ROWS_A])
                pe.transpose(scores[:, 2 * l, ROWS_A:N_ROWS], rows[0:ROWS_B, 2 * l + 1, :],
                             ident[0:ROWS_B, 0:ROWS_B]).then_inc(par_turned, 1)
            pe.wait_ge(x_loaded, 16)
            for pair in range(PAIRS):
                for i in range(2):
                    for s in range(ST):
                        ch = 2 * pair + i
                        ins = pe.transpose(stream[:, pair, SEQ * i + P * s:SEQ * i + P * (s + 1)],
                                           xtok[:, s, P * ch:P * (ch + 1)], ident)
                ins.then_inc(x_turned, 1)
            pe.wait_ge(par_copied, 1)
            pe.wait_ge(x_ready, PAIRS)

            with pe.Fori(0, DEPTH) as l:
                def adaln(a):
                    slot = POS["ada", a] % RAW_SLOTS
                    pe.wait_ge(raw_loaded[slot], at(raw_loaded[slot], l, RAW_READY["ada", a]))
                    w = raw[:, slot, :].rearrange("p (k m) -> p k m", k=8)
                    for t in range(4):
                        col = (4 * a + t) % 16
                        for k in range(8):
                            cc = COL["c"] + k
                            ins = pe.matmul(mod_ps[:, col:col + 1], w[:, k, P * t:P * (t + 1)], par[:, 0, cc:cc + 1],
                                            start=k == 0, stop=k == 7)
                    ins.then_inc(ada_done, 1)

                def three(ps, n, blk, hi, lo, first, last):
                    t = n % 4
                    wh = w_hi[:, t, P * blk:P * (blk + 1)]
                    wl = w_lo[:, t, P * blk:P * (blk + 1)]
                    pe.matmul(ps, wh, hi, start=first, stop=False)
                    pe.matmul(ps, wh, lo, start=False, stop=False)
                    return pe.matmul(ps, wl, hi, start=False, stop=last)

                def bank_wait(u, i):
                    b, use = BANK[u, i]
                    pe.wait_ge(bank_free[b], at(bank_free[b], l, use))

                def product(n, hi, lo, ready=None, per=1, base=0):
                    u, t = divmod(n, 4)
                    pe.wait_ge(wlo_ready, at(wlo_ready, l, n + 1))
                    if t % 2 == 0:
                        bank_wait(u, t // 2)
                    ps = pair_ps(u, t // 2)[:, t % 2, :]
                    for k in range(CT):
                        if ready is not None and k % per == 0:
                            pe.wait_ge(ready, at(ready, l, base + k // per + 1))
                        ins = three(ps, n, k, hi[:, k, :], lo[:, k, :], k == 0, k == CT - 1)
                    ins.then_inc(tile_done, 1)

                def rg_product(n):
                    u, t = divmod(n, 4)
                    half = t % 2
                    pe.wait_ge(wlo_ready, at(wlo_ready, l, n + 1))
                    for j in range(4):
                        if j % 2 == 0:
                            bank_wait(u, 2 * t + j // 2)
                        blk2, m = divmod(j, 2)
                        ps = pair_ps(u, 2 * t + j // 2)[:, j % 2, :]
                        for kt in range(2):
                            k = 4 * half + 2 * blk2 + kt
                            ins = three(ps, n, 4 * blk2 + 2 * kt + m, y_hi[:, k, :], y_lo[:, k, :], kt == 0, kt == 1)
                    ins.then_inc(tile_done, 1)

                def q_sum(i):
                    pe.wait_ge(q_squared, at(q_squared, l, i + 1))
                    if i >= 2:
                        pe.wait_ge(q_rstd, at(q_rstd, l, i - 1))
                    sq = tmp[:, 2 * (i % 2):2 * (i % 2) + 2, :].rearrange("p a b -> p (a b)")
                    pe.matmul(sums[i % 2], ones, sq, start=True, stop=True).then_inc(q_summed, 1)

                def q_rotate(i):
                    pe.wait_ge(q_normed, at(q_normed, l, i + 1))
                    if i >= 2:
                        pe.wait_ge(q_ready, at(q_ready, l, i - 1))
                    pe.matmul(turned[:, i % 2, :], rot, qkv[:, 2 * i:2 * i + 2, :].rearrange("p a b -> p (a b)"),
                              start=True, stop=True).then_inc(q_rotated, 1)

                def v_turn():
                    pe.wait_ge(bank_free[bank(U["kv", 0], 1)], freed_at(l, U["kv", 0], 1))
                    pe.wait_ge(q_ready, at(q_ready, l, 4))
                    for s in range(ST):
                        for j in range(N_KV):
                            o = (N_KV * s + j) * HD
                            ins = pe.transpose(turned[:, 1, o:o + HD], qkv[:, 10 + j, P * s:P * (s + 1)], ident)
                    ins.then_inc(v_turned, 1)

                def attention_scores(g):
                    if g == 0:
                        pe.wait_ge(q_ready, at(q_ready, l, 5))
                    else:
                        pe.wait_ge(exp_done, at(exp_done, l, g))
                    for i in range(2):
                        for s in range(ST):
                            ins = pe.matmul(scores[:, 2 * i + s, :], qkv[:, 2 * g + i, P * s:P * (s + 1)],
                                            qkv[:, 8 + g // 2, :], start=True, stop=True)
                    ins.then_inc(scored, 1)

                def attention_turn(g):
                    pe.wait_ge(probs_ready, at(probs_ready, l, g + 1))
                    if g == 0:
                        pe.wait_ge(v_ready, at(v_ready, l, 1))
                    else:
                        pe.wait_ge(o_ready, at(o_ready, l, g))
                    for s in range(ST):
                        for i in range(2):
                            for qs in range(ST):
                                o = SEQ * i + P * qs
                                ins = pe.transpose(turned[:, s, o:o + P], probs[:, 2 * i + qs, P * s:P * (s + 1)], ident)
                    ins.then_inc(probs_turned, 1)

                def attention_out(g):
                    pe.wait_ge(probsT_ready, at(probsT_ready, l, 2 * g + 2))
                    for s in range(ST):
                        ins = pe.matmul(turned[:, 0, :], vtok[:, s, g // 2, :], probsT[:, s, :], start=s == 0,
                                        stop=s == ST - 1)
                    ins.then_inc(o_summed, 1)

                adaln(0)
                adaln(1)
                for k in range(CT):
                    if k % 2 == 0:
                        pe.wait_ge(x_squared, at(x_squared, l, k // 2 + 1))
                    ins = pe.matmul(scores[:, 0, :], ones, buf_i[:, k, :], start=k == 0, stop=k == CT - 1)
                ins.then_inc(x_summed, 1)
                adaln(2)
                adaln(3)

                for n in range(NT):
                    u, t = divmod(n, 4)
                    name, part = UNITS[u]
                    if n in (12, 14, 16, 18, 20):
                        q_sum((n - 12) // 2)
                    if n in (15, 17, 19, 21, 23):
                        q_rotate((n - 15) // 2)
                    if n == 24:
                        v_turn()
                    if n in (68, 76, 84, 92):
                        attention_scores((n - 68) // 8)
                    if n in (73, 81, 89, 97):
                        attention_turn((n - 73) // 8)
                    if n in (76, 84, 92, 100):
                        attention_out((n - 76) // 8)
                    if n == 4 * U_OUT:
                        adaln(4)
                        adaln(5)
                    if name == "rg":
                        if n == 4 * U["rg", 0]:
                            pe.wait_ge(y_ready, at(y_ready, l, PAIRS))
                        rg_product(n)
                    elif name == "br":
                        first = t == 0 and part % 2 == 0
                        i = {BR_C: 1, BR_A: 2, BR_B: 3}[part // 2]
                        product(n, y_hi, y_lo, y_ready if first else None, 2, PAIRS * i)
                    elif name == "out":
                        product(n, h_hi, h_lo, y_ready if n == 4 * U_OUT else None, 2, PAIRS * 4)
                    else:
                        product(n, h_hi, h_lo, h_ready if n == 0 else None)

            for i in range(4):
                s, half = divmod(i, 2)
                if i == 0:
                    for pair in range(PAIRS):
                        pe.wait_ge(bank_free[bank(U_OUT + pair // 2, pair % 2)], freed_at(DEPTH - 1, U_OUT + pair // 2, pair % 2))
                for j in range(4):
                    ins = pe.transpose(stream[:, i, P * j:P * (j + 1)], xT[:, 4 * half + j, P * s:P * (s + 1)], ident)
                ins.then_inc(out_turned, 1)


def shape_constants():
    k = np.zeros((P, N_CONST), np.float32)
    k[:, C_ID:C_ID + P] = np.eye(P, dtype=np.float32)
    for m in range(P):
        if m % 64 < 32:
            k[m + 32, C_ROT + m] = -1.0
        else:
            k[m - 32, C_ROT + m] = 1.0
    k[:, C_ONE:C_ONE + P] = 1.0
    half = HD // 2
    inv = (np.float32(ROPE_THETA) ** (-np.arange(0, half, 2, dtype=np.float32) / np.float32(half))).astype(np.float32)
    tok = np.arange(SEQ)
    for p in range(P):
        at = (tok // GRID_W if p < half else tok % GRID_W).astype(np.float32)
        ang = (at * inv[p % 32]).astype(np.float32)
        for r in range(2):
            k[p, C_COS + SEQ * r:C_COS + SEQ * (r + 1)] = np.cos(ang)
            k[p, C_SIN + SEQ * r:C_SIN + SEQ * (r + 1)] = np.sin(ang)
    return k


_INS = ["x", "c", "w_ada", "b_ada", "norm_g", "w_in", "conv_a_w", "conv_a_b", "w_rg", "b_rg", "w_ig", "b_ig",
        "lru_lam", "q_norm_g", "k_norm_g", "conv_c_w", "w_branch", "w_out"]


def kernel(**inputs):
    import concourse.bacc as bacc
    from concourse.bass_utils import run_bass_kernel_spmd

    nc = bacc.Bacc("TRN2", target_bir_lowering=False, num_devices=1)
    arrays = {f"in_{name}": np.ascontiguousarray(inputs[name]) for name in _INS}
    arrays["consts"] = shape_constants()
    args = [nc.dram_tensor(n, a.shape, mybir.dt.from_np(a.dtype), kind="ExternalInput").ap() for n, a in arrays.items()]
    out = nc.dram_tensor("out", (1, SEQ, D), F32, kind="ExternalOutput").ap()
    trunk_program(nc, *args, out)
    result = run_bass_kernel_spmd(nc, [arrays], core_ids=[0])
    return result.results[0]["out"]
```

```python
from contextlib import ExitStack

import numpy as np

import concourse.bass as bass
from concourse import mybir

F32 = mybir.dt.float32
F32R = mybir.dt.float32r
ALU = mybir.AluOpType
ACT = mybir.ActivationFunctionType
AX_X = mybir.AxisListType.X

D = 1024
SEQ = 256
DEPTH = 2
P = 128
CT = D // P
PAIRS = CT // 2
ST = SEQ // P
N_HEADS, N_KV, HD = 8, 2, 128
RNN_BLOCKS, RNN_BW = 4, 256
CONV_A_W, CONV_A_LEFT = 4, 2
CONV_C_W, CONV_C_LEFT = 3, 1
N_BRANCH = 3
EPS = 1e-6
LRU_C = 8.0
GRID_W = 64
ROPE_THETA = 10000.0
SCALE = float(HD) ** -0.5

SIZES = dict(xa=D, ga=D, q=D, k=N_KV * HD, v=N_KV * HD, gb=D, xc=D, bc=D, cc=D, gc=D, mg=N_BRANCH * D)
COLUMN = {}
for _name in SIZES:
    COLUMN[_name] = sum(SIZES[m] for m in list(SIZES)[:list(SIZES).index(_name)])
N_IN = sum(SIZES.values())

BR_A, BR_B, BR_C = 0, 1, 2
UNITS = ([("xa", 0), ("xa", 1), ("q", 0), ("q", 1), ("kv", 0), ("rg", 0)]
         + [(n, 0) for n in ("xc", "cc", "bc", "gc")] + [("rg", 1)]
         + [(n, 1) for n in ("xc", "cc", "bc", "gc")]
         + [("mg", 2 * BR_C), ("mg", 2 * BR_C + 1), ("br", 2 * BR_C), ("br", 2 * BR_C + 1), ("ga", 0), ("ga", 1)]
         + [("mg", 2 * BR_A), ("mg", 2 * BR_A + 1), ("br", 2 * BR_A), ("br", 2 * BR_A + 1), ("gb", 0), ("gb", 1)]
         + [("mg", 2 * BR_B), ("mg", 2 * BR_B + 1), ("br", 2 * BR_B), ("br", 2 * BR_B + 1), ("out", 0), ("out", 1)])
NU = len(UNITS)
NT = 4 * NU
U = {name: i for i, name in enumerate(UNITS)}
U_OUT = U["out", 0]
NADA = 6
ADA_AFTER = {7: 0, 9: 1, 11: 2, 13: 3, 15: 4, 26: 5}
ADA_SUM_AT = {4 * u + 4: a for u, a in ADA_AFTER.items()}
RAW_SLOTS = 3


def load_plan(last):
    plan = []
    for u in range(NU):
        plan.append(("unit", u))
        if u in ADA_AFTER and not (last and ADA_AFTER[u] < 4):
            plan.append(("ada", ADA_AFTER[u]))
    return plan


def load_dmas(what):
    return 2 if what[0] == "unit" and UNITS[what[1]][0] == "rg" else 1


def raw_plan(plan):
    count, slot_of, ready = [0] * RAW_SLOTS, {}, {}
    for pos, what in enumerate(plan):
        slot_of[what] = pos % RAW_SLOTS
        count[pos % RAW_SLOTS] += 16 * load_dmas(what)
        ready[what] = count[pos % RAW_SLOTS]
    return slot_of, ready, count


PLAN = {last: load_plan(last) for last in (False, True)}
RAW = {last: raw_plan(PLAN[last]) for last in (False, True)}
RAW_COUNT = RAW[False][2]
assert len(PLAN[False]) % RAW_SLOTS == 0
ADA_ORDER = {last: [i for kind, i in PLAN[last] if kind == "ada"] for last in (False, True)}

BANKS = 4
BANK = {}
BANK_USES = [0] * BANKS
_b = 0
for _u, (_name, _) in enumerate(UNITS):
    for _i in range(8 if _name == "rg" else 2):
        BANK[_u, _i] = (_b % BANKS, BANK_USES[_b % BANKS])
        BANK_USES[_b % BANKS] += 1
        _b += 1

PARAMS = dict(norm_g=8, b_ada=24, conv_a_w=32, conv_a_b=8, b_rg=16, b_ig=16, lru_lam=16, conv_c_w=24,
              q_norm_g=1, k_norm_g=1, c=8)
COL = {}
for _name in PARAMS:
    COL[_name] = sum(PARAMS[m] for m in list(PARAMS)[:list(PARAMS).index(_name)])
N_ROWS = sum(PARAMS.values())
COL["pos8"] = N_ROWS
COL["neg8"] = N_ROWS + 16
COL["neg16"] = N_ROWS + 32
N_COLS = N_ROWS + 48

C_ID, C_ROT, C_ONE, C_COS, C_SIN = 0, P, 2 * P, 3 * P, 3 * P + 2 * SEQ
N_CONST = 3 * P + 4 * SEQ

MERGED_AT = (122, 124, 126, 127)

Q_SUM_AT = (12, 14, 17, 19, 21)
Q_ROTATE_AT = (18, 19, 22, 23, 24)
ROPE_AT = (21, 22, 25, 26, 27)
FIRST_SPLITS = 2

V_STEPS = 112
S_STEPS = 77


def trunk_program(nc, w_ada, w_in, w_rg, w_ig, w_branch, w_out, x, params, consts, out):
    w_in_v = w_in.rearrange("l (t p) n -> l p t n", p=P)
    w_ada_v = w_ada.rearrange("l (t p) n -> l p t n", p=P)
    w_br_v = w_branch.rearrange("l b (t p) n -> l b p t n", p=P)
    w_out_v = w_out.rearrange("l (t p) n -> l p t n", p=P)
    w_rg_v = w_rg.rearrange("l d n (t p) m -> l d p (n t) m", p=P)
    w_ig_v = w_ig.rearrange("l d n (t p) m -> l d p (n t) m", p=P)

    with ExitStack() as ctx:
        def sb(name, shape, dt=F32):
            return ctx.enter_context(nc.sbuf_tensor(name, shape, dt))

        def psum(name, shape):
            return ctx.enter_context(nc.psum_tensor(name, shape, F32))

        gain = {}

        def sem(name, per_layer=0, ahead=False, starts=0):
            s = ctx.enter_context(nc.semaphore(name))
            gain[id(s)] = (per_layer, per_layer if ahead else starts)
            return s

        def at(s, l, n):
            per_layer, start = gain[id(s)]
            return l * per_layer + (start + n)

        raw = sb("raw", [P, RAW_SLOTS, 8 * 512])
        w_hi = sb("w_hi", [P, 4, 8 * P], F32R)
        w_lo = sb("w_lo", [P, 4, 8 * P], F32R)
        xT = sb("xT", [P, CT, SEQ])
        h_hi = sb("h_hi", [P, CT, SEQ], F32R)
        h_lo = sb("h_lo", [P, CT, SEQ], F32R)
        y_hi = sb("y_hi", [P, CT, SEQ], F32R)
        y_lo = sb("y_lo", [P, CT, SEQ], F32R)
        padded = sb("padded", [P, CT, SEQ + 4])
        ua = sb("ua", [P, CT, SEQ])
        qkv = sb("qkv", [P, 12, SEQ])
        buf_i = sb("buf_i", [P, CT, SEQ])
        buf_r = sb("buf_r", [P, CT, SEQ])
        buf_t = sb("buf_t", [P, CT, SEQ])
        ya = sb("ya", [P, CT, SEQ])
        xc = sb("xc", [P, 4, SEQ])
        tmp = sb("tmp", [P, 4, SEQ])
        probs = sb("probs", [P, 4, SEQ])
        probsT = sb("probsT", [P, ST, 2 * SEQ])
        vtok = sb("vtok", [P, ST, N_KV, HD])
        cst = sb("cst", [P, N_CONST])
        par = sb("par", [P, DEPTH, N_COLS])
        cur = sb("cur", [P, N_COLS])
        rstd = sb("rstd", [P, SEQ])
        eps_t = sb("eps_t", [P, 1])
        eps_col = eps_t[:, 0:1]
        mods = sb("mods", [P, 4, CT])
        stat = sb("stat", [P, 4, 4])

        def yc(ch, n=1):
            if ch < 4:
                return padded[:, 4 + ch:4 + ch + n, CONV_A_LEFT:CONV_A_LEFT + SEQ]
            return ua[:, ch:ch + n, :]

        def whole(buffer):
            return lambda ch, n: buffer[:, ch:ch + n, :]

        yb = buf_t
        merged = buf_r
        gates = buf_i
        small = tmp[:, 0, 0:8 * 32].rearrange("p (a b) -> p a b", a=8)

        ident = cst[:, C_ID:C_ID + P]
        rot = cst[:, C_ROT:C_ROT + P]
        ones = cst[:, C_ONE:C_ONE + P]
        cos2 = cst[:, C_COS:C_COS + 2 * SEQ]
        sin2 = cst[:, C_SIN:C_SIN + 2 * SEQ]

        stream = psum("stream", [P, BANKS, 512])
        scores = psum("scores", [P, 4, SEQ])
        turned = psum("turned", [P, 2, 512])
        sums = [scores[:, 0:2, :].rearrange("p a b -> p (a b)"), scores[:, 2:4, :].rearrange("p a b -> p (a b)")]
        mod_ps = scores[:, 2, :]

        raw_loaded = [sem(f"raw_loaded{i}", RAW_COUNT[i], starts=16) for i in range(RAW_SLOTS)]
        whi_ready = sem("whi_ready", NT)
        wlo_ready = sem("wlo_ready", NT, ahead=True)
        tile_done = sem("tile_done", NT, ahead=True)
        bank_free = [sem(f"bank_free{b}", BANK_USES[b], ahead=True) for b in range(BANKS)]
        ada_summed = sem("ada_summed", NADA)
        ada_done = sem("ada_done", NADA)
        mods_part = sem("mods_part", NADA)
        x_squared = sem("x_squared", PAIRS)
        x_summed = sem("x_summed", 1)
        x_rstd = sem("x_rstd", 1)
        cur_ready = sem("cur_ready", 1)
        x_root = sem("x_root", 1)
        mods_ready = sem("mods_ready", 1, starts=1)
        x_gained = sem("x_gained", CT)
        hhi_ready = sem("hhi_ready", CT)
        h_ready = sem("h_ready", CT)
        ua_ready = sem("ua_ready", PAIRS)
        yhi_ready = sem("yhi_ready", 5 * PAIRS)
        y_ready = sem("y_ready", 5 * PAIRS)
        q_squared = sem("q_squared", 5)
        q_summed = sem("q_summed", 5)
        q_rstd = sem("q_rstd", 5)
        q_normed = sem("q_normed", 5)
        q_rotated = sem("q_rotated", 5)
        q_ready = sem("q_ready", 5)
        v_turned = sem("v_turned", 1)
        v_ready = sem("v_ready", 1)
        rg_exp = sem("rg_exp", 4)
        rg_w = sem("rg_w", 4)
        rg_root = sem("rg_root", 4)
        scanned = sem("scanned", 4)
        sigmoids = sem("sigmoids", 12)
        gated = sem("gated", 12)
        merged_ready = sem("merged_ready", PAIRS)
        scored = sem("scored", 4)
        max_ready = sem("max_ready", 4)
        exp_done = sem("exp_done", 4)
        probs_ready = sem("probs_ready", 4)
        probs_turned = sem("probs_turned", 4)
        probsT_ready = sem("probsT_ready", 8)
        o_summed = sem("o_summed", 4)
        o_ready = sem("o_ready", 4)
        p_step = sem("p_step", 9 * NADA)
        v_step = sem("v_step", V_STEPS)
        s_step = sem("s_step", S_STEPS)
        loaded = sem("loaded")
        first_ada = sem("first_ada")
        first_summed = sem("first_summed")
        first_done = sem("first_done")
        lam_exp = sem("lam_exp")
        v_first = sem("v_first")
        stored = sem("stored")

        class Steps:

            def __init__(self, step, l):
                self.step, self.l, self.n = step, l, 0

            def next(self):
                self.n += 1
                return 1

            def now(self, back=0):
                return at(self.step, self.l, self.n - back)

        def raw_tile(n, slot_of):
            u, t = divmod(n, 4)
            slot = slot_of["unit", u]
            if UNITS[u][0] == "rg":
                return raw[:, slot, 1024 * t:1024 * (t + 1)].rearrange("p (k m) -> p k m", k=8)
            return raw[:, slot, :].rearrange("p (k m) -> p k m", k=8)[:, :, P * t:P * (t + 1)]

        def pair_ps(u, i):
            return stream[:, BANK[u, i][0], :].rearrange("p (a b) -> p a b", a=2)

        def bank(u, i):
            return BANK[u, i][0]

        def freed_at(l, u, i, layers_back=0):
            b, use = BANK[u, i]
            return at(bank_free[b], l, use + 1 - layers_back * BANK_USES[b])

        block = ctx.enter_context(nc.Block())

        @block.sync
        def _(sync):
            for i in range(3):
                sync.dma_start(raw[:, i, :].rearrange("p (k m) -> p k m", k=8),
                               w_ada_v[0, :, :, 512 * i:512 * i + 512]).then_inc(raw_loaded[i], 16)
            for i, buffer in enumerate((buf_t, ya)):
                sync.dma_start(buffer[:, :, :].rearrange("p a b -> p (a b)").rearrange("p (k m) -> p k m", k=4),
                               w_ada_v[0, :, 4 * i:4 * i + 4, 1536:2048]).then_inc(first_ada, 16)

            def layer(l, last):
                slot_of = RAW[last][0]
                for pos, (kind, i) in enumerate(PLAN[last]):
                    slot = slot_of[kind, i]
                    if pos < RAW_SLOTS:
                        sync.wait_ge(first_done, pos + 1)
                        user, ui = PLAN[False][pos - RAW_SLOTS]
                        sync.wait_ge(wlo_ready, at(wlo_ready, l, 4 * ui + 4 - NT))
                    else:
                        user, ui = PLAN[last][pos - RAW_SLOTS]
                        if user == "unit":
                            sync.wait_ge(wlo_ready, at(wlo_ready, l, 4 * ui + 4))
                        else:
                            sync.wait_ge(ada_done, at(ada_done, l, ADA_ORDER[last].index(ui) + 1))
                    dst = raw[:, slot, :].rearrange("p (k m) -> p k m", k=8)
                    if kind == "ada":
                        src = w_ada_v[l + 1 if i < 4 else l, :, :, 512 * i:512 * i + 512]
                    else:
                        name, part = UNITS[i]
                        if name == "rg":
                            for gate, w in enumerate((w_rg_v, w_ig_v)):
                                sync.dma_start(raw[:, slot, 2048 * gate:2048 * (gate + 1)].rearrange(
                                    "p (k m) -> p k m", k=8), w[l, part]).then_inc(raw_loaded[slot], 16)
                            continue
                        if name == "br":
                            branch, half = divmod(part, 2)
                            src = w_br_v[l, branch, :, :, 512 * half:512 * half + 512]
                        elif name == "out":
                            src = w_out_v[l, :, :, 512 * part:512 * part + 512]
                        else:
                            col = COLUMN["k" if name == "kv" else name] + 512 * part
                            src = w_in_v[l, :, :, col:col + 512]
                    sync.dma_start(dst, src).then_inc(raw_loaded[slot], 16)

            with sync.Fori(0, DEPTH - 1) as l:
                layer(l, False)
            layer(DEPTH - 1, True)
            for pair in range(PAIRS):
                sync.wait_ge(bank_free[bank(U_OUT + pair // 2, pair % 2)],
                             freed_at(DEPTH - 1, U_OUT + pair // 2, pair % 2))
                sync.dma_start(out[:, 2 * pair:2 * pair + 2, :], xT[:, 2 * pair:2 * pair + 2, :]).then_inc(stored, 16)
            sync.wait_ge(stored, 16 * PAIRS)

        @block.scalar
        def _(act):
            act.dma_start(par[:, :, 0:N_ROWS], params).then_inc(loaded, 16)
            act.dma_start(xT[:], x).then_inc(loaded, 16)
            act.dma_start(cst[:], consts).then_inc(loaded, 16)
            lam = par[:, :, COL["lru_lam"]:COL["lru_lam"] + 16]
            e_l = small[:, 0, :].rearrange("p (a b) -> p a b", a=DEPTH)
            act.wait_ge(loaded, 48)
            act.activation(e_l, lam, ACT.Abs).then_inc(lam_exp, 1)
            act.wait_ge(lam_exp, 1)
            act.activation(e_l, e_l, ACT.Exp, scale=-1.0).then_inc(lam_exp, 1)
            act.wait_ge(v_first, 2)

            def layer(l, last):
                slot_of, raw_ready = RAW[last][:2]
                own = Steps(s_step, l)

                def split_hi(n):
                    u, t = divmod(n, 4)
                    if t == 0:
                        slot = slot_of["unit", u]
                        act.wait_ge(raw_loaded[slot], at(raw_loaded[slot], l, raw_ready["unit", u]))
                    act.wait_ge(tile_done, at(tile_done, l, n - 3))
                    act.activation(w_hi[:, t, :].rearrange("p (k m) -> p k m", k=8), raw_tile(n, slot_of),
                                   ACT.Copy).then_inc(whi_ready, 1)

                def split_y(i, pair, src, dst):
                    act.activation(dst[:, 2 * pair:2 * pair + 2, :], src(2 * pair, 2),
                                   ACT.Copy).then_inc(yhi_ready, 1)

                def squares(i):
                    u, pair = U["q", 0] + i // 2, i % 2
                    ps = pair_ps(u, pair)
                    if i >= 2 and i < 5:
                        act.wait_ge(q_summed, at(q_summed, l, i - 1))
                    if i < 5:
                        act.activation(tmp[:, 2 * (i % 2):2 * (i % 2) + 2, :], ps, ACT.Square).then_inc(q_squared, 1)
                    act.activation(qkv[:, 2 * i:2 * i + 2, :], ps, ACT.Copy).then_inc(bank_free[bank(u, pair)], 1)

                def q_norm(pairs):
                    r = probs[:, :, :].rearrange("p (i a) b -> p i (a b)", i=2)
                    for i in pairs:
                        act.wait_ge(q_summed, at(q_summed, l, i + 1))
                        if i >= 2:
                            act.wait_ge(q_normed, at(q_normed, l, i - 1))
                        act.activation(r[:, i % 2, :], sums[i % 2], ACT.Ln, bias=eps_col,
                                       scale=1.0 / HD).then_inc(s_step, own.next())
                    act.wait_ge(s_step, own.now())
                    for i in pairs:
                        act.activation(r[:, i % 2, :], r[:, i % 2, :], ACT.Exp, scale=-0.5).then_inc(q_rstd, 1)

                def rg_sigmoids(d, t):
                    u = U["rg", d]
                    kind, half = divmod(t, 2)
                    if d == 1 and t == 0:
                        act.wait_ge(scanned, at(scanned, l, 2))
                    dst, bias = (buf_r, "b_rg") if kind == 0 else (buf_i, "b_ig")
                    for j in range(4):
                        ch = 4 * half + j
                        col = COL[bias] + 8 * d + ch
                        ins = act.activation(dst[:, ch, :], pair_ps(u, 2 * t + j // 2)[:, j % 2, :],
                                             ACT.Sigmoid, bias=cur[:, col:col + 1])
                        if j % 2:
                            ins.then_inc(bank_free[bank(u, 2 * t + j // 2)], 1)
                        else:
                            ins.then_inc(s_step, own.next())

                def rg_scaled(d, half, dst, func, coef):
                    for j in range(4):
                        ch = 4 * half + j
                        col = COL[coef] + 8 * d + ch
                        ins = act.activation(dst(ch), buf_r[:, ch, :], func, scale=cur[:, col:col + 1])
                        if j < 3 or coef != "neg16":
                            ins.then_inc(s_step, own.next())
                        else:
                            ins.then_inc(rg_exp, 1)

                def rg_math(d, s):
                    if s in (0, 3):
                        half = s // 3
                        act.wait_ge(bank_free[bank(U["rg", d], 2 * half + 1)], freed_at(l, U["rg", d], 2 * half + 1))
                        rg_scaled(d, half, lambda ch: buf_t[:, ch, :], ACT.Tanh, "pos8")
                    elif s in (1, 4):
                        half = s // 3
                        if half == 1 or d == 1:
                            act.wait_ge(rg_w, at(rg_w, l, 2 * d + half))
                        rg_scaled(d, half, lambda ch: tmp[:, ch % 4, :], ACT.Exp, "neg16")
                    elif s in (2, 5):
                        rg_scaled(d, s // 3, lambda ch: buf_r[:, ch, :], ACT.Exp, "neg8")
                    else:
                        half = s - 6
                        act.wait_ge(rg_w, at(rg_w, l, 2 * d + half + 1))
                        t4 = buf_t[:, 4 * half:4 * half + 4, :]
                        act.activation(t4, t4, ACT.Sqrt).then_inc(rg_root, 1)

                def silu_sigmoid(i, u, pair):
                    slot = i % 2
                    if i >= 2:
                        act.wait_ge(gated, at(gated, l, i - 1))
                    act.activation(xc[:, 2 * slot:2 * slot + 2, :], pair_ps(u, pair),
                                   ACT.Sigmoid).then_inc(sigmoids, 1)

                def softmax_exp(g):
                    act.wait_ge(max_ready, at(max_ready, l, g + 1))
                    if g:
                        act.wait_ge(probs_turned, at(probs_turned, l, g))
                    for j in range(4):
                        ins = act.activation(probs[:, j, :], scores[:, j, :], ACT.Exp, bias=stat[:, 1, j:j + 1],
                                             scale=SCALE, accum_out=stat[:, 2, j:j + 1])
                        if j < 3:
                            ins.then_inc(s_step, own.next())
                    ins.then_inc(exp_done, 1)

                def probs_out(g):
                    act.wait_ge(probs_turned, at(probs_turned, l, g + 1))
                    if g:
                        act.wait_ge(o_summed, at(o_summed, l, g))
                    for s in range(ST):
                        act.activation(probsT[:, s, :], turned[:, s, :], ACT.Copy).then_inc(probsT_ready, 1)

                def consume(u, pair):
                    name, part = UNITS[u]
                    act.wait_ge(tile_done, at(tile_done, l, 4 * u + 2 * pair + 2))
                    ps = pair_ps(u, pair)
                    if name == "xa":
                        ch = 4 * part + 2 * pair
                        act.activation(padded[:, ch:ch + 2, CONV_A_LEFT:CONV_A_LEFT + SEQ], ps, ACT.Copy).then_inc(bank_free[bank(u, pair)], 1)
                    elif name in ("q", "kv"):
                        i = 2 * (u - U["q", 0]) + pair
                        squares(i)
                    elif name == "xc":
                        if part == 1:
                            act.wait_ge(gated, at(gated, l, pair + 1))
                        act.activation(xc[:, 2 * pair:2 * pair + 2, :], ps, ACT.Copy).then_inc(bank_free[bank(u, pair)], 1)
                    elif name == "gc":
                        act.wait_ge(bank_free[bank(U["cc", part], pair)], freed_at(l, U["cc", part], pair))
                        act.activation(xc[:, 2 * pair:2 * pair + 2, :], ps, ACT.Sigmoid).then_inc(sigmoids, 1)
                    elif name in ("ga", "gb"):
                        silu_sigmoid((4 if name == "ga" else 8) + 2 * part + pair, u, pair)
                    elif name == "mg":
                        ch = 4 * (part % 2) + 2 * pair
                        act.activation(gates[:, ch:ch + 2, :], ps, ACT.Sigmoid).then_inc(bank_free[bank(u, pair)], 1)

                for pair in range(PAIRS):
                    act.wait_ge(bank_free[bank(U_OUT + pair // 2, pair % 2)],
                                freed_at(l, U_OUT + pair // 2, pair % 2, layers_back=1))
                    act.activation(buf_i[:, 2 * pair:2 * pair + 2, :], xT[:, 2 * pair:2 * pair + 2, :],
                                   ACT.Square).then_inc(x_squared, 1)
                act.wait_ge(x_summed, at(x_summed, l, 1))
                act.activation(rstd[:], scores[:, 0, :], ACT.Sqrt, bias=eps_col, scale=1.0 / D).then_inc(x_root, 1)
                for n in range(FIRST_SPLITS):
                    split_hi(n)
                for k in range(CT):
                    act.wait_ge(x_gained, at(x_gained, l, k + 1))
                    act.activation(h_hi[:, k, :], buf_r[:, k, :], ACT.Identity,
                                   bias=mods[:, 0, k:k + 1]).then_inc(hhi_ready, 1)
                for n in range(FIRST_SPLITS, 4):
                    split_hi(n)

                for n in range(4, NT):
                    u, t = divmod(n, 4)
                    split_hi(n)
                    if UNITS[u - 1][0] == "rg":
                        act.wait_ge(tile_done, at(tile_done, l, 4 * (u - 1) + t + 1))
                        rg_sigmoids(UNITS[u - 1][1], t)
                    elif t % 2:
                        consume(u - 1, t // 2)
                    if n in (6, 8, 10, 12):
                        i = (n - 6) // 2
                        act.wait_ge(ua_ready, at(ua_ready, l, i + 1))
                        split_y(0, i, whole(ua), y_hi)
                    if n in (18, 22, 23):
                        q_norm({18: (0, 1), 22: (2, 3), 23: (4,)}[n])
                    if 28 <= n < 36:
                        rg_math(0, n - 28)
                    if 48 <= n < 56:
                        rg_math(1, n - 48)
                    if n in (64, 65, 66, 67):
                        act.wait_ge(gated, at(gated, l, n - 63))
                        split_y(1, n - 64, yc, y_hi)
                    if n in (72, 80, 88, 96):
                        softmax_exp((n - 72) // 8)
                    if n in (76, 84, 92, 100):
                        probs_out((n - 76) // 8)
                    if n in (82, 84, 86, 88):
                        i = (n - 82) // 2
                        act.wait_ge(gated, at(gated, l, 5 + i))
                        split_y(2, i, whole(ya), y_hi)
                    if n in (106, 108, 110, 112):
                        i = (n - 106) // 2
                        act.wait_ge(gated, at(gated, l, 9 + i))
                        split_y(3, i, whole(yb), y_hi)
                    if n in MERGED_AT:
                        i = MERGED_AT.index(n)
                        act.wait_ge(merged_ready, at(merged_ready, l, i + 1))
                        split_y(4, i, whole(merged), h_hi)
                assert own.n == S_STEPS, own.n

            with act.Fori(0, DEPTH - 1) as l:
                layer(l, False)
            layer(DEPTH - 1, True)

        @block.vector
        def _(vec):
            vec.memset(padded[:, :, :], 0.0).then_inc(v_first, 1)
            vec.memset(eps_col, EPS).then_inc(v_first, 1)
            vec.sem_inc(wlo_ready, NT)
            for b in range(BANKS):
                vec.sem_inc(bank_free[b], BANK_USES[b])

            def first_sum(a):
                if a < 3:
                    vec.wait_ge(raw_loaded[a], 16)
                    blocks = [raw[:, a, 512 * k:512 * k + 512] for k in range(8)]
                else:
                    vec.wait_ge(first_ada, 32)
                    blocks = [t[:, 2 * k:2 * k + 2, :].rearrange("p a b -> p (a b)") for t in (buf_t, ya) for k in range(4)]
                for k in range(8):
                    ck = par[:, 0, COL["c"] + k:COL["c"] + k + 1]
                    if k < 2:
                        ins = vec.tensor_scalar(blocks[k], blocks[k], ck, None, ALU.mult)
                    else:
                        vec.wait_ge(v_first, done[0] - 1)
                        ins = vec.scalar_tensor_tensor(out=blocks[k % 2], in0=blocks[k], scalar=ck, in1=blocks[k % 2],
                                                       op0=ALU.mult, op1=ALU.add)
                    if k < 7:
                        ins.then_inc(v_first, 1)
                        done[0] += 1
                ins.then_inc(first_summed, 1)

            vec.wait_ge(loaded, 48)
            lam = par[:, :, COL["lru_lam"]:COL["lru_lam"] + 16]

            def scratch(i):
                return small[:, i, :].rearrange("p (a b) -> p a b", a=DEPTH)

            e_l, s_l, s2, q_l, sp = (scratch(i) for i in range(5))
            done = [2]

            def chain(instruction):
                instruction.then_inc(v_first, 1)
                done[0] += 1
                vec.wait_ge(v_first, done[0])

            vec.wait_ge(lam_exp, 2)
            chain(vec.tensor_scalar(s_l, e_l, 2.0, None, ALU.add))
            chain(vec.reciprocal(s_l, s_l))
            chain(vec.tensor_tensor(s_l, s_l, e_l, ALU.mult))
            chain(vec.tensor_tensor(s2, s_l, s_l, ALU.mult))
            chain(vec.tensor_scalar(q_l, s2, 1.0 / 15, None, ALU.mult))
            for odd in (13, 11, 9, 7, 5, 3):
                chain(vec.scalar_tensor_tensor(out=q_l, in0=q_l, scalar=1.0 / odd, in1=s2, op0=ALU.add, op1=ALU.mult))
            chain(vec.scalar_tensor_tensor(out=q_l, in0=q_l, scalar=1.0, in1=s_l, op0=ALU.add, op1=ALU.mult))
            chain(vec.tensor_scalar(sp, lam, -1.0, 0.0, ALU.mult, ALU.max))
            chain(vec.scalar_tensor_tensor(out=sp, in0=q_l, scalar=2.0, in1=sp, op0=ALU.mult, op1=ALU.add))
            for name, factor in (("pos8", LRU_C), ("neg8", -LRU_C), ("neg16", -2 * LRU_C)):
                chain(vec.tensor_scalar(par[:, :, COL[name]:COL[name] + 16], sp, factor, None, ALU.mult))
            for a in range(4):
                first_sum(a)
            vec.wait_ge(first_done, 4)
            chain(vec.tensor_tensor(mods[:, 0:2, :], mod_ps[:, 0:16].rearrange("p (a b) -> p a b", a=2),
                                    par[:, 0, COL["b_ada"]:COL["b_ada"] + 16].rearrange("p (a b) -> p a b", a=2),
                                    ALU.add))
            vec.scalar_tensor_tensor(out=mods[:, 2, :], in0=mods[:, 1, :], scalar=1.0,
                                     in1=par[:, 0, COL["norm_g"]:COL["norm_g"] + 8], op0=ALU.add,
                                     op1=ALU.mult).then_inc(mods_ready, 1)

            def layer(l, last):
                slot_of = RAW[last][0]
                own = Steps(v_step, l)

                def split_lo(n):
                    t = n % 4
                    vec.wait_ge(whi_ready, at(whi_ready, l, n + 1))
                    vec.tensor_tensor(w_lo[:, t, :].rearrange("p (k m) -> p k m", k=8), raw_tile(n, slot_of),
                                      w_hi[:, t, :].bitcast(F32).rearrange("p (k m) -> p k m", k=8),
                                      ALU.subtract).then_inc(wlo_ready, 1)

                def h_low(k):
                    vec.wait_ge(hhi_ready, at(hhi_ready, l, k + 1))
                    vec.scalar_tensor_tensor(out=h_lo[:, k, :], in0=buf_r[:, k, :], scalar=mods[:, 0, k:k + 1],
                                             in1=h_hi[:, k, :].bitcast(F32), op0=ALU.add,
                                             op1=ALU.subtract).then_inc(h_ready, 1)

                def ada_part(a):
                    order = ADA_ORDER[last].index(a) + 1
                    vec.wait_ge(ada_done, at(ada_done, l, order))
                    b = COL["b_ada"] + 4 * a
                    src = cur[:, b:b + 4] if a >= 4 else par[:, bass.ds(l + 1, 1), b:b + 4].rearrange("p a b -> p (a b)")
                    dst = mods[:, (0, 1, 3)[a // 2], 4 * (a % 2):4 * (a % 2) + 4]
                    vec.tensor_tensor(dst, mod_ps[:, 4 * a:4 * a + 4], src, ALU.add).then_inc(mods_part, 1)
                    if a == 3:
                        vec.wait_ge(mods_part, at(mods_part, l, order))
                        g = COL["norm_g"]
                        vec.scalar_tensor_tensor(out=mods[:, 2, :], in0=mods[:, 1, :], scalar=1.0,
                                                 in1=par[:, bass.ds(l + 1, 1), g:g + 8].rearrange("p a b -> p (a b)"),
                                                 op0=ALU.add, op1=ALU.mult).then_inc(mods_ready, 1)

                def split_y(i, pair, src, hi, lo):
                    vec.wait_ge(yhi_ready, at(yhi_ready, l, PAIRS * i + pair + 1))
                    s = slice(2 * pair, 2 * pair + 2)
                    vec.tensor_tensor(lo[:, s, :], src(2 * pair, 2), hi[:, s, :].bitcast(F32),
                                      ALU.subtract).then_inc(y_ready, 1)

                def conv(pair, src, shift0, taps, weight, bias, dst, src_tile, signal=None):
                    chs = (2 * pair, 2 * pair + 1)
                    for k in range(taps):
                        for i, ch in enumerate(chs):
                            win = src[:, src_tile + i, shift0 + k:shift0 + k + SEQ]
                            col = COL[weight] + 8 * k + ch
                            wk = cur[:, col:col + 1]
                            if k == 0:
                                b = cur[:, COL[bias] + ch:COL[bias] + ch + 1] if bias else None
                                ins = vec.tensor_scalar(dst(ch, 1)[:, 0, :], win, wk, b, ALU.mult,
                                                        ALU.add if bias else ALU.bypass)
                            else:
                                vec.wait_ge(v_step, own.now(back=1))
                                ins = vec.scalar_tensor_tensor(out=dst(ch, 1)[:, 0, :], in0=win, scalar=wk,
                                                               in1=dst(ch, 1)[:, 0, :], op0=ALU.mult, op1=ALU.add)
                            if signal is not None and k == taps - 1 and i == 1:
                                ins.then_inc(signal, 1)
                            else:
                                ins.then_inc(v_step, own.next())

                def q_norm(i):
                    vec.wait_ge(q_rstd, at(q_rstd, l, i + 1))
                    g = COL["q_norm_g" if i < 4 else "k_norm_g"]
                    z = qkv[:, 2 * i:2 * i + 2, :]
                    vec.scalar_tensor_tensor(out=z, in0=z, scalar=cur[:, g:g + 1],
                                             in1=probs[:, 2 * (i % 2):2 * (i % 2) + 2, :], op0=ALU.mult,
                                             op1=ALU.mult).then_inc(q_normed, 1)

                def rope(i):
                    vec.wait_ge(q_rotated, at(q_rotated, l, i + 1))
                    z = qkv[:, 2 * i:2 * i + 2, :].rearrange("p a b -> p (a b)")
                    r = probsT[:, i % 2, :]
                    vec.tensor_tensor(r, turned[:, i % 2, :], sin2, ALU.mult).then_inc(v_step, own.next())
                    vec.tensor_tensor(z, z, cos2, ALU.mult).then_inc(v_step, own.next())
                    vec.wait_ge(v_step, own.now())
                    vec.tensor_tensor(z, z, r, ALU.add).then_inc(q_ready, 1)

                def rg_math(d, s):
                    if s in (0, 3):
                        half = s // 3
                        vec.wait_ge(bank_free[bank(U["rg", d], 4 + 2 * half + 1)], freed_at(l, U["rg", d], 4 + 2 * half + 1))
                        z = buf_i[:, 4 * half:4 * half + 4, :]
                        vec.tensor_tensor(z, z, ua_of(half), ALU.mult).then_inc(v_step, own.next())
                    if s in (2, 5):
                        half = (s - 2) // 3
                        vec.wait_ge(rg_exp, at(rg_exp, l, 2 * d + half + 1))
                        t4 = buf_t[:, 4 * half:4 * half + 4, :]
                        vec.scalar_tensor_tensor(out=t4.rearrange("p a b -> p (a b)"),
                                                 in0=tmp[:, :, :].rearrange("p a b -> p (a b)"), scalar=1.0,
                                                 in1=t4.rearrange("p a b -> p (a b)"), op0=ALU.add,
                                                 op1=ALU.mult).then_inc(rg_w, 1)
                    if s in (9, 10):
                        half = s - 9
                        vec.wait_ge(rg_root, at(rg_root, l, 2 * d + half + 1))
                        z = buf_i[:, 4 * half:4 * half + 4, :]
                        vec.tensor_tensor(z, z, buf_t[:, 4 * half:4 * half + 4, :], ALU.mult).then_inc(v_step, own.next())
                    if s in (11, 12):
                        half = s - 11
                        vec.wait_ge(v_step, own.now())
                        for j in range(4):
                            ch = 4 * half + j
                            a, u_, o = buf_r[:, ch, :], buf_i[:, ch, :], (ya if d == 0 else buf_t)[:, ch, :]
                            if d == 1:
                                a, u_, o = a[:, ::-1], u_[:, ::-1], o[:, ::-1]
                            ins = vec.tensor_tensor_scan(o, a, u_, 0.0, ALU.mult, ALU.add)
                            if j < 3:
                                ins.then_inc(v_step, own.next())
                            else:
                                ins.then_inc(scanned, 1)
                    if d == 1 and s in (13, 14):
                        half = s - 13
                        vec.wait_ge(scanned, at(scanned, l, 3 + half))
                        z = ya[:, 4 * half:4 * half + 4, :]
                        vec.tensor_tensor(z, z, buf_t[:, 4 * half:4 * half + 4, :], ALU.add).then_inc(v_step, own.next())

                def ua_of(half):
                    return ua[:, 4 * half:4 * half + 4, :]

                def silu_gate(i, u, pair, y, ch):
                    vec.wait_ge(sigmoids, at(sigmoids, l, i + 1))
                    z = xc[:, 2 * (i % 2):2 * (i % 2) + 2, :]
                    vec.tensor_tensor(z, z, pair_ps(u, pair), ALU.mult).then_inc(bank_free[bank(u, pair)], 1)
                    vec.wait_ge(bank_free[bank(u, pair)], freed_at(l, u, pair))
                    vec.tensor_tensor(y(ch, 2), y(ch, 2), z, ALU.mult).then_inc(gated, 1)

                def softmax_max(g):
                    vec.wait_ge(scored, at(scored, l, g + 1))
                    vec.tensor_reduce(stat[:, 0, :], scores[:, :, :], AX_X, ALU.max).then_inc(v_step, own.next())
                    vec.wait_ge(v_step, own.now())
                    vec.tensor_scalar(stat[:, 1, :], stat[:, 0, :], -SCALE, None, ALU.mult).then_inc(max_ready, 1)

                def softmax_norm(g):
                    vec.wait_ge(exp_done, at(exp_done, l, g + 1))
                    vec.reciprocal(stat[:, 3, :], stat[:, 2, :]).then_inc(v_step, own.next())
                    vec.wait_ge(v_step, own.now())
                    for j in range(4):
                        ins = vec.tensor_scalar(probs[:, j, :], probs[:, j, :], stat[:, 3, j:j + 1], None, ALU.mult)
                        if j < 3:
                            ins.then_inc(v_step, own.next())
                    ins.then_inc(probs_ready, 1)

                def consume(u, pair):
                    name, part = UNITS[u]
                    ps = pair_ps(u, pair)
                    if name == "xa":
                        vec.wait_ge(bank_free[bank(u, pair)], freed_at(l, u, pair))
                        ch = 4 * part + 2 * pair
                        conv(ch // 2, padded, 0, CONV_A_W, "conv_a_w", "conv_a_b", whole(ua), ch, signal=ua_ready)
                    elif name == "cc":
                        vec.wait_ge(tile_done, at(tile_done, l, 4 * u + 2 * pair + 2))
                        vec.wait_ge(bank_free[bank(U["xc", part], pair)], freed_at(l, U["xc", part], pair))
                        vec.tensor_tensor(padded[:, 2 * pair:2 * pair + 2, CONV_A_LEFT:CONV_A_LEFT + SEQ], ps,
                                                xc[:, 2 * pair:2 * pair + 2, :], ALU.mult).then_inc(bank_free[bank(u, pair)], 1)
                    elif name == "bc":
                        vec.wait_ge(tile_done, at(tile_done, l, 4 * u + 2 * pair + 2))
                        vec.wait_ge(v_step, own.now())
                        ch = 4 * part + 2 * pair
                        vec.tensor_tensor(yc(ch, 2), yc(ch, 2), ps, ALU.mult).then_inc(bank_free[bank(u, pair)], 1)
                    elif name == "gc":
                        silu_gate(2 * part + pair, u, pair, yc, 4 * part + 2 * pair)
                    elif name == "ga":
                        silu_gate(4 + 2 * part + pair, u, pair, whole(ya), 4 * part + 2 * pair)
                    elif name == "gb":
                        silu_gate(8 + 2 * part + pair, u, pair, whole(yb), 4 * part + 2 * pair)
                    elif name == "br":
                        branch, half = divmod(part, 2)
                        ch = 4 * half + 2 * pair
                        vec.wait_ge(tile_done, at(tile_done, l, 4 * u + 2 * pair + 2))
                        vec.wait_ge(bank_free[bank(U["mg", part], pair)], freed_at(l, U["mg", part], pair))
                        m, g = merged[:, ch:ch + 2, :], gates[:, ch:ch + 2, :]
                        if branch == BR_C:
                            vec.tensor_tensor(m, g, ps, ALU.mult).then_inc(bank_free[bank(u, pair)], 1)
                        else:
                            z = tmp[:, 2 * pair:2 * pair + 2, :]
                            vec.tensor_tensor(z, g, ps, ALU.mult).then_inc(bank_free[bank(u, pair)], 1)
                            vec.wait_ge(bank_free[bank(u, pair)], freed_at(l, u, pair))
                            ins = vec.tensor_tensor(m, m, z, ALU.add)
                            if branch == BR_B:
                                ins.then_inc(merged_ready, 1)
                            else:
                                ins.then_inc(v_step, own.next())
                    elif name == "out":
                        vec.wait_ge(tile_done, at(tile_done, l, 4 * u + 2 * pair + 2))
                        vec.wait_ge(mods_part, at(mods_part, l, len(ADA_ORDER[last])))
                        for i in range(2):
                            ch = 4 * part + 2 * pair + i
                            ins = vec.scalar_tensor_tensor(out=xT[:, ch, :], in0=ps[:, i, :],
                                                           scalar=mods[:, 3, ch:ch + 1], in1=xT[:, ch, :],
                                                           op0=ALU.mult, op1=ALU.add)
                            if i == 0:
                                ins.then_inc(v_step, own.next())
                        ins.then_inc(bank_free[bank(u, pair)], 1)

                vec.tensor_copy(cur[:], par[:, bass.ds(l, 1), :].rearrange("p a b -> p (a b)")).then_inc(cur_ready, 1)
                vec.wait_ge(x_root, at(x_root, l, 1))
                vec.reciprocal(rstd[:], rstd[:]).then_inc(x_rstd, 1)
                vec.wait_ge(x_rstd, at(x_rstd, l, 1))
                vec.wait_ge(mods_ready, at(mods_ready, l, 0))
                for k in range(CT):
                    vec.scalar_tensor_tensor(out=buf_r[:, k, :], in0=xT[:, k, :], scalar=mods[:, 2, k:k + 1],
                                             in1=rstd[:], op0=ALU.mult, op1=ALU.mult).then_inc(x_gained, 1)
                    if k >= 1:
                        h_low(k - 1)
                    if k == 4:
                        split_lo(0)
                h_low(CT - 1)
                for n in range(1, 4):
                    split_lo(n)

                for n in range(4, NT):
                    u, t = divmod(n, 4)
                    split_lo(n)
                    if UNITS[u - 1][0] != "rg" and t % 2:
                        consume(u - 1, t // 2)
                    if n in (6, 8, 10, 12):
                        split_y(0, (n - 6) // 2, whole(ua), y_hi, y_lo)
                    if n in (18, 22):
                        q_norm((n - 18) // 2)
                        q_norm((n - 18) // 2 + 1)
                    if n == 23:
                        q_norm(4)
                    if n in ROPE_AT:
                        rope(ROPE_AT.index(n))
                    if n - 3 in ADA_SUM_AT and ADA_SUM_AT[n - 3] in ADA_ORDER[last]:
                        ada_part(ADA_SUM_AT[n - 3])
                    if n == 30:
                        vec.wait_ge(v_turned, at(v_turned, l, 1))
                        vec.tensor_copy(vtok[:, :, :, :].rearrange("p a b c -> p (a b c)"),
                                        turned[:, 1, :]).then_inc(v_ready, 1)
                    for d, start in ((0, 28), (1, 48)):
                        if start <= n < start + 15:
                            rg_math(d, n - start)
                    for part, start in ((0, 34), (1, 54)):
                        if n in (start, start + 2):
                            pair = (n - start) // 2
                            vec.wait_ge(bank_free[bank(U["cc", part], pair)], freed_at(l, U["cc", part], pair))
                            conv(2 * part + pair, padded, CONV_A_LEFT - CONV_C_LEFT, CONV_C_W, "conv_c_w", None,
                                 yc, 2 * pair)
                    if n in (64, 65, 66, 67):
                        split_y(1, n - 64, yc, y_hi, y_lo)
                    if n in (72, 80, 88, 96):
                        softmax_max((n - 72) // 8)
                    if n in (73, 81, 89, 97):
                        softmax_norm((n - 73) // 8)
                    if n in (80, 88, 96, 104):
                        g = (n - 80) // 8
                        vec.wait_ge(o_summed, at(o_summed, l, g + 1))
                        vec.tensor_copy(yb[:, 2 * g:2 * g + 2, :],
                                        turned[:, 0, :].rearrange("p (a b) -> p a b", a=2)).then_inc(o_ready, 1)
                    if n in (82, 84, 86, 88):
                        split_y(2, (n - 82) // 2, whole(ya), y_hi, y_lo)
                    if n in (106, 108, 110, 112):
                        split_y(3, (n - 106) // 2, whole(yb), y_hi, y_lo)
                    if n in MERGED_AT:
                        split_y(4, MERGED_AT.index(n), whole(merged), h_hi, h_lo)
                for pair in range(2):
                    consume(NU - 1, pair)
                assert own.n == V_STEPS, own.n

            with vec.Fori(0, DEPTH - 1) as l:
                layer(l, False)
            layer(DEPTH - 1, True)

        @block.gpsimd
        def _(pool):
            pool.wait_ge(loaded, 48)

            def layer(l, last):
                slot_of, raw_ready = RAW[last][:2]
                own = Steps(p_step, l)
                for a in ADA_ORDER[last]:
                    slot = slot_of["ada", a]
                    w = raw[:, slot, :]
                    pool.wait_ge(raw_loaded[slot], at(raw_loaded[slot], l, raw_ready["ada", a]))
                    for k in range(8):
                        col = COL["c"] + k
                        pool.tensor_scalar(w[:, 512 * k:512 * k + 512], w[:, 512 * k:512 * k + 512],
                                           par[:, 0, col:col + 1], 1.0, ALU.mult, ALU.mult).then_inc(p_step, own.next())
                    pool.wait_ge(p_step, own.now())
                    pool.tensor_tensor(w[:, 0:2048], w[:, 0:2048], w[:, 2048:4096],
                                       ALU.add).then_inc(p_step, own.next())
                    pool.wait_ge(p_step, own.now())
                    pool.tensor_tensor(w[:, 0:1024], w[:, 0:1024], w[:, 1024:2048],
                                       ALU.add).then_inc(ada_summed, 1)

            with pool.Fori(0, DEPTH - 1) as l:
                layer(l, False)
            layer(DEPTH - 1, True)

        @block.tensor
        def _(pe):
            pe.sem_inc(tile_done, NT)

            def column_sums(w, col):
                for t in range(4):
                    for half in range(2):
                        o = 512 * half + P * t
                        ins = pe.matmul(mod_ps[:, col + t:col + t + 1], w(o), ones[:, 0:1], start=half == 0,
                                        stop=half == 1)
                return ins

            pe.wait_ge(loaded, 48)
            for a in range(3):
                pe.wait_ge(first_summed, a + 1)
                column_sums(lambda o: raw[:, a, o:o + P], 4 * a).then_inc(first_done, 1)
            pe.wait_ge(first_summed, 4)
            column_sums(lambda o: buf_t[:, :, :].rearrange("p a b -> p (a b)")[:, o:o + P], 12).then_inc(first_done, 1)

            def layer(l, last):
                slot_of = RAW[last][0]

                def adaln(a):
                    slot = slot_of["ada", a]
                    order = ADA_ORDER[last].index(a)
                    pe.wait_ge(ada_summed, at(ada_summed, l, order + 1))
                    if order:
                        pe.wait_ge(mods_part, at(mods_part, l, order))
                    column_sums(lambda o: raw[:, slot, o:o + P], 4 * a).then_inc(ada_done, 1)

                def three(ps, n, blk, hi, lo, first, last):
                    t = n % 4
                    wh = w_hi[:, t, P * blk:P * (blk + 1)]
                    wl = w_lo[:, t, P * blk:P * (blk + 1)]
                    pe.matmul(ps, wh, hi, start=first, stop=False)
                    pe.matmul(ps, wh, lo, start=False, stop=False)
                    return pe.matmul(ps, wl, hi, start=False, stop=last)

                def bank_wait(u, i):
                    b, use = BANK[u, i]
                    pe.wait_ge(bank_free[b], at(bank_free[b], l, use))

                def product(n, hi, lo, ready=None, per=1, base=0):
                    u, t = divmod(n, 4)
                    pe.wait_ge(wlo_ready, at(wlo_ready, l, n + 1))
                    if t % 2 == 0:
                        bank_wait(u, t // 2)
                    ps = pair_ps(u, t // 2)[:, t % 2, :]
                    for k in range(CT):
                        if ready is not None and k % per == 0:
                            pe.wait_ge(ready, at(ready, l, base + k // per + 1))
                        ins = three(ps, n, k, hi[:, k, :], lo[:, k, :], k == 0, k == CT - 1)
                    ins.then_inc(tile_done, 1)

                def rg_product(n):
                    u, t = divmod(n, 4)
                    half = t % 2
                    pe.wait_ge(wlo_ready, at(wlo_ready, l, n + 1))
                    for j in range(4):
                        if j % 2 == 0:
                            bank_wait(u, 2 * t + j // 2)
                        blk2, m = divmod(j, 2)
                        ps = pair_ps(u, 2 * t + j // 2)[:, j % 2, :]
                        for kt in range(2):
                            k = 4 * half + 2 * blk2 + kt
                            ins = three(ps, n, 4 * blk2 + 2 * kt + m, y_hi[:, k, :], y_lo[:, k, :], kt == 0, kt == 1)
                    ins.then_inc(tile_done, 1)

                def q_sum(i):
                    pe.wait_ge(q_squared, at(q_squared, l, i + 1))
                    if i >= 2:
                        pe.wait_ge(q_rstd, at(q_rstd, l, i - 1))
                    sq = tmp[:, 2 * (i % 2):2 * (i % 2) + 2, :].rearrange("p a b -> p (a b)")
                    pe.matmul(sums[i % 2], ones, sq, start=True, stop=True).then_inc(q_summed, 1)

                def q_rotate(i):
                    pe.wait_ge(q_normed, at(q_normed, l, i + 1))
                    if i >= 2:
                        pe.wait_ge(q_ready, at(q_ready, l, i - 1))
                    pe.matmul(turned[:, i % 2, :], rot, qkv[:, 2 * i:2 * i + 2, :].rearrange("p a b -> p (a b)"),
                              start=True, stop=True).then_inc(q_rotated, 1)

                def v_turn():
                    pe.wait_ge(bank_free[bank(U["kv", 0], 1)], freed_at(l, U["kv", 0], 1))
                    pe.wait_ge(q_ready, at(q_ready, l, 4))
                    for s in range(ST):
                        for j in range(N_KV):
                            o = (N_KV * s + j) * HD
                            ins = pe.transpose(turned[:, 1, o:o + HD], qkv[:, 10 + j, P * s:P * (s + 1)], ident)
                    ins.then_inc(v_turned, 1)

                def attention_scores(g):
                    if g == 0:
                        pe.wait_ge(q_ready, at(q_ready, l, 5))
                        pe.wait_ge(mods_part, at(mods_part, l, len(ADA_ORDER[last]) - 1))
                    else:
                        pe.wait_ge(exp_done, at(exp_done, l, g))
                    for i in range(2):
                        for s in range(ST):
                            ins = pe.matmul(scores[:, 2 * i + s, :], qkv[:, 2 * g + i, P * s:P * (s + 1)],
                                            qkv[:, 8 + g // 2, :], start=True, stop=True)
                    ins.then_inc(scored, 1)

                def attention_turn(g):
                    pe.wait_ge(probs_ready, at(probs_ready, l, g + 1))
                    if g == 0:
                        pe.wait_ge(v_ready, at(v_ready, l, 1))
                    else:
                        pe.wait_ge(o_ready, at(o_ready, l, g))
                    for s in range(ST):
                        for i in range(2):
                            for qs in range(ST):
                                o = SEQ * i + P * qs
                                ins = pe.transpose(turned[:, s, o:o + P], probs[:, 2 * i + qs, P * s:P * (s + 1)], ident)
                    ins.then_inc(probs_turned, 1)

                def attention_out(g):
                    pe.wait_ge(probsT_ready, at(probsT_ready, l, 2 * g + 2))
                    for s in range(ST):
                        ins = pe.matmul(turned[:, 0, :], vtok[:, s, g // 2, :], probsT[:, s, :], start=s == 0,
                                        stop=s == ST - 1)
                    ins.then_inc(o_summed, 1)

                for k in range(CT):
                    if k % 2 == 0:
                        pe.wait_ge(x_squared, at(x_squared, l, k // 2 + 1))
                    ins = pe.matmul(scores[:, 0, :], ones, buf_i[:, k, :], start=k == 0, stop=k == CT - 1)
                ins.then_inc(x_summed, 1)

                for n in range(NT):
                    u, t = divmod(n, 4)
                    name, part = UNITS[u]
                    if n in Q_SUM_AT:
                        q_sum(Q_SUM_AT.index(n))
                    if n in Q_ROTATE_AT:
                        q_rotate(Q_ROTATE_AT.index(n))
                    if n == 26:
                        v_turn()
                    if n in (68, 76, 84, 92):
                        attention_scores((n - 68) // 8)
                    if n in (73, 81, 89, 97):
                        attention_turn((n - 73) // 8)
                    if n in (76, 84, 92, 100):
                        attention_out((n - 76) // 8)
                    if n in ADA_SUM_AT and ADA_SUM_AT[n] in ADA_ORDER[last]:
                        adaln(ADA_SUM_AT[n])
                    if name == "rg":
                        if n == 4 * U["rg", 0]:
                            pe.wait_ge(y_ready, at(y_ready, l, PAIRS))
                        rg_product(n)
                    elif name == "br":
                        first = t == 0 and part % 2 == 0
                        i = {BR_C: 1, BR_A: 2, BR_B: 3}[part // 2]
                        product(n, y_hi, y_lo, y_ready if first else None, 2, PAIRS * i)
                    elif name == "out":
                        product(n, h_hi, h_lo, y_ready if n == 4 * U_OUT else None, 2, PAIRS * 4)
                    else:
                        product(n, h_hi, h_lo, h_ready if n == 0 else None)

            with pe.Fori(0, DEPTH - 1) as l:
                layer(l, False)
            layer(DEPTH - 1, True)


def shape_constants():
    k = np.zeros((P, N_CONST), np.float32)
    k[:, C_ID:C_ID + P] = np.eye(P, dtype=np.float32)
    for m in range(P):
        if m % 64 < 32:
            k[m + 32, C_ROT + m] = -1.0
        else:
            k[m - 32, C_ROT + m] = 1.0
    k[:, C_ONE:C_ONE + P] = 1.0
    half = HD // 2
    inv = (np.float32(ROPE_THETA) ** (-np.arange(0, half, 2, dtype=np.float32) / np.float32(half))).astype(np.float32)
    tok = np.arange(SEQ)
    for p in range(P):
        at = (tok // GRID_W if p < half else tok % GRID_W).astype(np.float32)
        ang = (at * inv[p % 32]).astype(np.float32)
        for r in range(2):
            k[p, C_COS + SEQ * r:C_COS + SEQ * (r + 1)] = np.cos(ang)
            k[p, C_SIN + SEQ * r:C_SIN + SEQ * (r + 1)] = np.sin(ang)
    return k


def packed_params(inputs):
    rows = []
    for layer in range(DEPTH):
        for name, n in PARAMS.items():
            a = inputs[name][0] if name == "c" else inputs[name][layer]
            rows.append(np.reshape(a, (n, P)))
    return np.ascontiguousarray(np.concatenate(rows).reshape(DEPTH, N_ROWS, P).transpose(2, 0, 1))


def kernel(**inputs):
    import concourse.bacc as bacc
    from concourse.bass_utils import run_bass_kernel_spmd

    inputs = {name: np.asarray(a) for name, a in inputs.items()}
    nc = bacc.Bacc("TRN2", target_bir_lowering=False, num_devices=1)
    arrays = {name: np.ascontiguousarray(inputs[name]) for name in ("w_ada", "w_in", "w_rg", "w_ig", "w_branch", "w_out")}
    arrays["x"] = np.ascontiguousarray(inputs["x"][0].reshape(SEQ, CT, P).transpose(2, 1, 0))
    arrays["params"] = packed_params(inputs)
    arrays["consts"] = shape_constants()
    args = [nc.dram_tensor(f"in_{n}", a.shape, mybir.dt.from_np(a.dtype), kind="ExternalInput").ap()
            for n, a in arrays.items()]
    out = nc.dram_tensor("out", (P, CT, SEQ), F32, kind="ExternalOutput").ap()
    trunk_program(nc, *args, out)
    result = run_bass_kernel_spmd(nc, [{f"in_{n}": a for n, a in arrays.items()}], core_ids=[0])
    return np.ascontiguousarray(result.results[0]["out"].transpose(2, 1, 0)).reshape(1, SEQ, D)
```

```python
from contextlib import ExitStack

import numpy as np

import concourse.bass as bass
from concourse import mybir

F32 = mybir.dt.float32
F32R = mybir.dt.float32r
ALU = mybir.AluOpType
ACT = mybir.ActivationFunctionType
AX_X = mybir.AxisListType.X

D = 1024
SEQ = 256
DEPTH = 2
P = 128
CT = D // P
PAIRS = CT // 2
ST = SEQ // P
N_HEADS, N_KV, HD = 8, 2, 128
RNN_BLOCKS, RNN_BW = 4, 256
CONV_A_W, CONV_A_LEFT = 4, 2
CONV_C_W, CONV_C_LEFT = 3, 1
N_BRANCH = 3
EPS = 1e-6
LRU_C = 8.0
GRID_W = 64
ROPE_THETA = 10000.0
SCALE = float(HD) ** -0.5

SIZES = dict(xa=D, ga=D, q=D, k=N_KV * HD, v=N_KV * HD, gb=D, xc=D, bc=D, cc=D, gc=D, mg=N_BRANCH * D)
COLUMN = {}
for _name in SIZES:
    COLUMN[_name] = sum(SIZES[m] for m in list(SIZES)[:list(SIZES).index(_name)])
N_IN = sum(SIZES.values())

BR_A, BR_B, BR_C = 0, 1, 2
UNITS = ([("xa", 0), ("xa", 1), ("q", 0), ("q", 1), ("kv", 0), ("rg", 0)]
         + [(n, 0) for n in ("xc", "cc", "bc", "gc")] + [("rg", 1)]
         + [(n, 1) for n in ("xc", "cc", "bc", "gc")]
         + [("mg", 2 * BR_C), ("mg", 2 * BR_C + 1), ("br", 2 * BR_C), ("br", 2 * BR_C + 1), ("ga", 0), ("ga", 1)]
         + [("mg", 2 * BR_A), ("mg", 2 * BR_A + 1), ("br", 2 * BR_A), ("br", 2 * BR_A + 1), ("gb", 0), ("gb", 1)]
         + [("mg", 2 * BR_B), ("mg", 2 * BR_B + 1), ("br", 2 * BR_B), ("br", 2 * BR_B + 1), ("out", 0), ("out", 1)])
NU = len(UNITS)
NT = 4 * NU
U = {name: i for i, name in enumerate(UNITS)}
U_OUT = U["out", 0]
ADA_AFTER = {7: 4, 9: 5, 22: 0, 24: 1, 26: 2, 28: 3}
GATE_AT = 54
RAW_SLOTS = 3


def load_plan(last):
    plan = []
    for u in range(NU):
        plan.append(("unit", u))
        if u in ADA_AFTER and not (last and ADA_AFTER[u] < 4):
            plan.append(("ada", ADA_AFTER[u]))
    return plan


def load_dmas(what):
    return 2 if what == ("unit", 0) or (what[0] == "unit" and UNITS[what[1]][0] == "rg") else 1


def raw_plan(plan):
    count, slot_of, ready = [0] * RAW_SLOTS, {}, {}
    for pos, what in enumerate(plan):
        slot_of[what] = pos % RAW_SLOTS
        count[pos % RAW_SLOTS] += 16 * load_dmas(what)
        ready[what] = count[pos % RAW_SLOTS]
    return slot_of, ready, count


PLAN = {last: load_plan(last) for last in (False, True)}
RAW = {last: raw_plan(PLAN[last]) for last in (False, True)}
RAW_COUNT = RAW[False][2]
assert len(PLAN[False]) % RAW_SLOTS == 0

BANKS = 4
BANK = {}
BANK_USES = [0] * BANKS
_b = 0
for _u, (_name, _) in enumerate(UNITS):
    for _i in range(8 if _name == "rg" else 2):
        BANK[_u, _i] = (_b % BANKS, BANK_USES[_b % BANKS])
        BANK_USES[_b % BANKS] += 1
        _b += 1



def place(n):
    u, t = divmod(n, 4)
    return u, (0, 2, 1, 3)[t] if u == 0 else t


def tiles_for(u, pair):
    return 3 if (u, pair) == (0, 0) else 4 * u + 2 * pair + 2


PARAMS = dict(norm_g=8, b_ada=24, conv_a_w=32, conv_a_b=8, b_rg=16, b_ig=16, lru_lam=16, conv_c_w=24,
              q_norm_g=1, k_norm_g=1, c=8)
COL = {}
for _name in PARAMS:
    COL[_name] = sum(PARAMS[m] for m in list(PARAMS)[:list(PARAMS).index(_name)])
N_ROWS = sum(PARAMS.values())
COL["pos8"] = N_ROWS
COL["neg8"] = N_ROWS + 16
COL["neg16"] = N_ROWS + 32
N_COLS = N_ROWS + 48

C_ID, C_ROT, C_COS, C_SIN = 0, P, 2 * P, 2 * P + 2 * SEQ
N_CONST = 2 * P + 4 * SEQ

MERGED_AT = (122, 124, 126, 127)

Q_SUM_AT = (12, 14, 17, 19, 21)
Q_ROTATE_AT = (19, 20, 24, 25, 26)
ROPE_AT = (22, 23, 27, 28, 29)
V_TURN_AT, V_COPY_AT = 32, 35
FIRST_SPLITS = 2

V_STEPS = 112
S_STEPS = 77


def trunk_program(nc, w_ada, w_in, w_rg, w_ig, w_branch, w_out, x, params, consts, out):
    w_in_v = w_in.rearrange("l (t p) n -> l p t n", p=P)
    w_ada_v = w_ada.rearrange("l (t p) n -> l p t n", p=P)
    w_br_v = w_branch.rearrange("l b (t p) n -> l b p t n", p=P)
    w_out_v = w_out.rearrange("l (t p) n -> l p t n", p=P)
    w_rg_v = w_rg.rearrange("l d n (t p) m -> l d p (n t) m", p=P)
    w_ig_v = w_ig.rearrange("l d n (t p) m -> l d p (n t) m", p=P)

    with ExitStack() as ctx:
        def sb(name, shape, dt=F32):
            return ctx.enter_context(nc.sbuf_tensor(name, shape, dt))

        def psum(name, shape):
            return ctx.enter_context(nc.psum_tensor(name, shape, F32))

        gain = {}

        def sem(name, per_layer=0, ahead=False, starts=0):
            s = ctx.enter_context(nc.semaphore(name))
            gain[id(s)] = (per_layer, per_layer if ahead else starts)
            return s

        def at(s, l, n):
            per_layer, start = gain[id(s)]
            return l * per_layer + (start + n)

        raw = sb("raw", [P, RAW_SLOTS, 8 * 512])
        w_hi = sb("w_hi", [P, 4, 8 * P], F32R)
        w_lo = sb("w_lo", [P, 4, 8 * P], F32R)
        xT = sb("xT", [P, CT, SEQ])
        h_hi = sb("h_hi", [P, CT, SEQ], F32R)
        h_lo = sb("h_lo", [P, CT, SEQ], F32R)
        y_hi = sb("y_hi", [P, CT, SEQ], F32R)
        y_lo = sb("y_lo", [P, CT, SEQ], F32R)
        padded = sb("padded", [P, CT, SEQ + 4])
        ua = sb("ua", [P, CT, SEQ])
        qkv = sb("qkv", [P, 12, SEQ])
        buf_i = sb("buf_i", [P, CT, SEQ])
        buf_r = sb("buf_r", [P, CT, SEQ])
        buf_t = sb("buf_t", [P, CT, SEQ])
        ya = sb("ya", [P, CT, SEQ])
        xc = sb("xc", [P, 4, SEQ])
        tmp = sb("tmp", [P, 4, SEQ])
        probs = sb("probs", [P, 4, SEQ])
        probsT = sb("probsT", [P, ST, 2 * SEQ])
        vtok = sb("vtok", [P, ST, N_KV, HD])
        cst = sb("cst", [P, N_CONST])
        ones = sb("ones", [P, P])[:, :]
        par = sb("par", [P, DEPTH, N_COLS])
        cur = sb("cur", [P, N_COLS])
        rstd = sb("rstd", [P, SEQ])
        eps_t = sb("eps_t", [P, 1])
        warm = sb("warm", [P, 1])
        eps_col = eps_t[:, 0:1]
        mods = sb("mods", [P, 4, CT])
        stat = sb("stat", [P, 4, 4])

        def yc(ch, n=1):
            if ch < 4:
                return padded[:, 4 + ch:4 + ch + n, CONV_A_LEFT:CONV_A_LEFT + SEQ]
            return ua[:, ch:ch + n, :]

        def whole(buffer):
            return lambda ch, n: buffer[:, ch:ch + n, :]

        yb = buf_t
        merged = buf_r
        gates = buf_i
        small = tmp[:, 0, 0:8 * 32].rearrange("p (a b) -> p a b", a=8)

        next_sums = [qkv[:, 2 * a:2 * a + 2, :].rearrange("p a b -> p (a b)") for a in range(4)]
        gate_sums = [probs[:, 2 * i:2 * i + 2, :].rearrange("p a b -> p (a b)") for i in range(2)]

        ident = cst[:, C_ID:C_ID + P]
        rot = cst[:, C_ROT:C_ROT + P]
        cos2 = cst[:, C_COS:C_COS + 2 * SEQ]
        sin2 = cst[:, C_SIN:C_SIN + 2 * SEQ]

        stream = psum("stream", [P, BANKS, 512])
        scores = psum("scores", [P, 4, SEQ])
        turned = psum("turned", [P, 2, 512])
        sums = [scores[:, 0:2, :].rearrange("p a b -> p (a b)"), scores[:, 2:4, :].rearrange("p a b -> p (a b)")]
        mod_ps = scores[:, 2, :]

        raw_loaded = [sem(f"raw_loaded{i}", RAW_COUNT[i], starts=16) for i in range(RAW_SLOTS)]
        half_loaded = sem("half_loaded", 32)
        whi_ready = sem("whi_ready", NT)
        wlo_ready = sem("wlo_ready", NT, ahead=True)
        tile_done = sem("tile_done", NT, ahead=True)
        bank_free = [sem(f"bank_free{b}", BANK_USES[b], ahead=True) for b in range(BANKS)]
        next_summed = sem("next_summed", 4)
        gate_summed = sem("gate_summed", 2)
        next_done = sem("next_done", 1)
        gate_done = sem("gate_done", 1)
        gate_ready = sem("gate_ready", 1)
        x_squared = sem("x_squared", PAIRS)
        x_summed = sem("x_summed", 1)
        x_rstd = sem("x_rstd", 1)
        cur_ready = sem("cur_ready", 1)
        x_root = sem("x_root", 1)
        mods_ready = sem("mods_ready", 2)
        x_gained = sem("x_gained", CT)
        hhi_ready = sem("hhi_ready", CT)
        h_ready = sem("h_ready", CT)
        ua_ready = sem("ua_ready", PAIRS)
        yhi_ready = sem("yhi_ready", 5 * PAIRS)
        y_ready = sem("y_ready", 5 * PAIRS)
        q_squared = sem("q_squared", 5)
        q_summed = sem("q_summed", 5)
        q_rstd = sem("q_rstd", 5)
        q_normed = sem("q_normed", 5)
        q_rotated = sem("q_rotated", 5)
        q_ready = sem("q_ready", 5)
        v_turned = sem("v_turned", 1)
        v_ready = sem("v_ready", 1)
        rg_exp = sem("rg_exp", 4)
        rg_w = sem("rg_w", 4)
        rg_root = sem("rg_root", 4)
        scanned = sem("scanned", 4)
        sigmoids = sem("sigmoids", 12)
        gated = sem("gated", 12)
        merged_ready = sem("merged_ready", PAIRS)
        scored = sem("scored", 4)
        max_ready = sem("max_ready", 4)
        exp_done = sem("exp_done", 4)
        probs_ready = sem("probs_ready", 4)
        probs_turned = sem("probs_turned", 4)
        probsT_ready = sem("probsT_ready", 8)
        o_summed = sem("o_summed", 4)
        o_ready = sem("o_ready", 4)
        p_step = sem("p_step", 10 * len(ADA_AFTER))
        v_step = sem("v_step", V_STEPS)
        s_warm = sem("s_warm", 1)
        s_step = sem("s_step", S_STEPS)
        params_loaded = sem("params_loaded")
        x_loaded = sem("x_loaded")
        consts_loaded = sem("consts_loaded")
        first_ada = [sem(f"first_ada{i}") for i in range(2)]
        lam_exp = sem("lam_exp")
        v_first = sem("v_first")
        stored = sem("stored")

        class Steps:

            def __init__(self, step, l):
                self.step, self.l, self.n = step, l, 0

            def next(self):
                self.n += 1
                return 1

            def now(self, back=0):
                return at(self.step, self.l, self.n - back)

        def raw_tile(n, slot_of):
            u, t = place(n)
            slot = slot_of["unit", u]
            if UNITS[u][0] == "rg":
                return raw[:, slot, 1024 * t:1024 * (t + 1)].rearrange("p (k m) -> p k m", k=8)
            return raw[:, slot, :].rearrange("p (k m) -> p k m", k=8)[:, :, P * t:P * (t + 1)]

        def pair_ps(u, i):
            return stream[:, BANK[u, i][0], :].rearrange("p (a b) -> p a b", a=2)

        def bank(u, i):
            return BANK[u, i][0]

        def freed_at(l, u, i, layers_back=0):
            b, use = BANK[u, i]
            return at(bank_free[b], l, use + 1 - layers_back * BANK_USES[b])

        block = ctx.enter_context(nc.Block())

        @block.sync
        def _(sync):
            sync.dma_start(par[:, :, 0:N_ROWS], params).then_inc(params_loaded, 16)
            for i in range(3):
                sync.dma_start(raw[:, i, :].rearrange("p (k m) -> p k m", k=8),
                               w_ada_v[0, :, :, 512 * i:512 * i + 512]).then_inc(raw_loaded[i], 16)
            sync.dma_start(xT[:], x).then_inc(x_loaded, 16)
            for i, buffer in enumerate((buf_t, ya)):
                sync.dma_start(buffer[:, :, :].rearrange("p a b -> p (a b)").rearrange("p (k m) -> p k m", k=4),
                               w_ada_v[0, :, 4 * i:4 * i + 4, 1536:2048]).then_inc(first_ada[i], 16)

            def layer(l, last):
                slot_of = RAW[last][0]
                for pos, (kind, i) in enumerate(PLAN[last]):
                    slot = slot_of[kind, i]
                    if pos < RAW_SLOTS:
                        sync.wait_ge(next_summed, pos + 1)
                        user, ui = PLAN[False][pos - RAW_SLOTS]
                        sync.wait_ge(wlo_ready, at(wlo_ready, l, 4 * ui + 4 - NT))
                    else:
                        user, ui = PLAN[last][pos - RAW_SLOTS]
                        if user == "unit":
                            sync.wait_ge(wlo_ready, at(wlo_ready, l, 4 * ui + 4))
                        elif ui >= 4:
                            sync.wait_ge(gate_summed, at(gate_summed, l, ui - 3))
                        else:
                            sync.wait_ge(next_summed, at(next_summed, l + 1, ui + 1))
                    dst = raw[:, slot, :].rearrange("p (k m) -> p k m", k=8)
                    if kind == "ada":
                        src = w_ada_v[l + 1 if i < 4 else l, :, :, 512 * i:512 * i + 512]
                    else:
                        name, part = UNITS[i]
                        if name == "rg":
                            for gate, w in enumerate((w_rg_v, w_ig_v)):
                                sync.dma_start(raw[:, slot, 2048 * gate:2048 * (gate + 1)].rearrange(
                                    "p (k m) -> p k m", k=8), w[l, part]).then_inc(raw_loaded[slot], 16)
                            continue
                        if name == "br":
                            branch, half = divmod(part, 2)
                            src = w_br_v[l, branch, :, :, 512 * half:512 * half + 512]
                        elif name == "out":
                            src = w_out_v[l, :, :, 512 * part:512 * part + 512]
                        else:
                            col = COLUMN["k" if name == "kv" else name] + 512 * part
                            src = w_in_v[l, :, :, col:col + 512]
                    if (kind, i) == ("unit", 0):
                        for n in range(4):
                            c = P * place(n)[1]
                            landed = half_loaded if n < 2 else raw_loaded[slot]
                            sync.dma_start(dst[:, :, c:c + P], src[:, :, c:c + P]).then_inc(landed, 16)
                    else:
                        sync.dma_start(dst, src).then_inc(raw_loaded[slot], 16)

            with sync.Fori(0, DEPTH - 1) as l:
                layer(l, False)
            layer(DEPTH - 1, True)
            for pair in range(PAIRS):
                sync.wait_ge(bank_free[bank(U_OUT + pair // 2, pair % 2)],
                             freed_at(DEPTH - 1, U_OUT + pair // 2, pair % 2))
                sync.dma_start(out[:, 2 * pair:2 * pair + 2, :], xT[:, 2 * pair:2 * pair + 2, :]).then_inc(stored, 16)
            sync.wait_ge(stored, 16 * PAIRS)

        @block.scalar
        def _(act):
            lam = par[:, :, COL["lru_lam"]:COL["lru_lam"] + 16]
            e_l = small[:, 0, :].rearrange("p (a b) -> p a b", a=DEPTH)
            act.wait_ge(params_loaded, 16)
            act.activation(e_l, lam, ACT.Abs).then_inc(lam_exp, 1)
            act.wait_ge(lam_exp, 1)
            act.activation(e_l, e_l, ACT.Exp, scale=-1.0).then_inc(lam_exp, 1)
            act.wait_ge(v_first, 2)

            def split_hi(l, n, last=False):
                slot_of, raw_ready = RAW[last][:2]
                u, t = divmod(n, 4)
                if n == 0:
                    act.wait_ge(half_loaded, at(half_loaded, l, 32))
                elif n == 2 or t == 0:
                    slot = slot_of["unit", u]
                    act.wait_ge(raw_loaded[slot], at(raw_loaded[slot], l, raw_ready["unit", u]))
                act.wait_ge(tile_done, at(tile_done, l, n - 3))
                act.activation(w_hi[:, t, :].rearrange("p (k m) -> p k m", k=8), raw_tile(n, slot_of),
                               ACT.Copy).then_inc(whi_ready, 1)

            def square(l, pair):
                act.wait_ge(bank_free[bank(U_OUT + pair // 2, pair % 2)],
                            freed_at(l, U_OUT + pair // 2, pair % 2, layers_back=1))
                act.activation(buf_i[:, 2 * pair:2 * pair + 2, :], xT[:, 2 * pair:2 * pair + 2, :],
                               ACT.Square).then_inc(x_squared, 1)

            def root_mean_square(l):
                act.wait_ge(x_summed, at(x_summed, l, 1))
                act.activation(rstd[:], scores[:, 0, :], ACT.Sqrt, bias=eps_col, scale=1.0 / D).then_inc(x_root, 1)

            act.activation(warm[:], eps_col, ACT.Sqrt).then_inc(s_warm, 1)
            act.wait_ge(x_loaded, 16)
            for pair in range(PAIRS):
                square(0, pair)
            root_mean_square(0)
            for n in range(FIRST_SPLITS):
                split_hi(0, n)

            def layer(l, last):
                own = Steps(s_step, l)

                def split_y(i, pair, src, dst):
                    act.activation(dst[:, 2 * pair:2 * pair + 2, :], src(2 * pair, 2),
                                   ACT.Copy).then_inc(yhi_ready, 1)

                def squares(i):
                    u, pair = U["q", 0] + i // 2, i % 2
                    ps = pair_ps(u, pair)
                    if i >= 2 and i < 5:
                        act.wait_ge(q_summed, at(q_summed, l, i - 1))
                    if i < 5:
                        act.activation(tmp[:, 2 * (i % 2):2 * (i % 2) + 2, :], ps, ACT.Square).then_inc(q_squared, 1)
                    act.activation(qkv[:, 2 * i:2 * i + 2, :], ps, ACT.Copy).then_inc(bank_free[bank(u, pair)], 1)

                def q_norm(pairs):
                    r = probs[:, :, :].rearrange("p (i a) b -> p i (a b)", i=2)
                    for i in pairs:
                        act.wait_ge(q_summed, at(q_summed, l, i + 1))
                        if i >= 2:
                            act.wait_ge(q_normed, at(q_normed, l, i - 1))
                        act.activation(r[:, i % 2, :], sums[i % 2], ACT.Ln, bias=eps_col,
                                       scale=1.0 / HD).then_inc(s_step, own.next())
                    act.wait_ge(s_step, own.now())
                    for i in pairs:
                        act.activation(r[:, i % 2, :], r[:, i % 2, :], ACT.Exp, scale=-0.5).then_inc(q_rstd, 1)

                def rg_sigmoids(d, t):
                    u = U["rg", d]
                    kind, half = divmod(t, 2)
                    if d == 1 and t == 0:
                        act.wait_ge(scanned, at(scanned, l, 2))
                    dst, bias = (buf_r, "b_rg") if kind == 0 else (buf_i, "b_ig")
                    for j in range(4):
                        ch = 4 * half + j
                        col = COL[bias] + 8 * d + ch
                        ins = act.activation(dst[:, ch, :], pair_ps(u, 2 * t + j // 2)[:, j % 2, :],
                                             ACT.Sigmoid, bias=cur[:, col:col + 1])
                        if j % 2:
                            ins.then_inc(bank_free[bank(u, 2 * t + j // 2)], 1)
                        else:
                            ins.then_inc(s_step, own.next())

                def rg_scaled(d, half, dst, func, coef):
                    for j in range(4):
                        ch = 4 * half + j
                        col = COL[coef] + 8 * d + ch
                        ins = act.activation(dst(ch), buf_r[:, ch, :], func, scale=cur[:, col:col + 1])
                        if j < 3 or coef != "neg16":
                            ins.then_inc(s_step, own.next())
                        else:
                            ins.then_inc(rg_exp, 1)

                def rg_math(d, s):
                    if s in (0, 3):
                        half = s // 3
                        act.wait_ge(bank_free[bank(U["rg", d], 2 * half + 1)], freed_at(l, U["rg", d], 2 * half + 1))
                        rg_scaled(d, half, lambda ch: buf_t[:, ch, :], ACT.Tanh, "pos8")
                    elif s in (1, 4):
                        half = s // 3
                        if half == 1 or d == 1:
                            act.wait_ge(rg_w, at(rg_w, l, 2 * d + half))
                        rg_scaled(d, half, lambda ch: tmp[:, ch % 4, :], ACT.Exp, "neg16")
                    elif s in (2, 5):
                        rg_scaled(d, s // 3, lambda ch: buf_r[:, ch, :], ACT.Exp, "neg8")
                    else:
                        half = s - 6
                        act.wait_ge(rg_w, at(rg_w, l, 2 * d + half + 1))
                        t4 = buf_t[:, 4 * half:4 * half + 4, :]
                        act.activation(t4, t4, ACT.Sqrt).then_inc(rg_root, 1)

                def silu_sigmoid(i, u, pair):
                    slot = i % 2
                    if i >= 2:
                        act.wait_ge(gated, at(gated, l, i - 1))
                    act.activation(xc[:, 2 * slot:2 * slot + 2, :], pair_ps(u, pair),
                                   ACT.Sigmoid).then_inc(sigmoids, 1)

                def softmax_exp(g):
                    act.wait_ge(max_ready, at(max_ready, l, g + 1))
                    if g:
                        act.wait_ge(probs_turned, at(probs_turned, l, g))
                    for j in range(4):
                        ins = act.activation(probs[:, j, :], scores[:, j, :], ACT.Exp, bias=stat[:, 1, j:j + 1],
                                             scale=SCALE, accum_out=stat[:, 2, j:j + 1])
                        if j < 3:
                            ins.then_inc(s_step, own.next())
                    ins.then_inc(exp_done, 1)

                def probs_out(g):
                    act.wait_ge(probs_turned, at(probs_turned, l, g + 1))
                    if g:
                        act.wait_ge(o_summed, at(o_summed, l, g))
                    for s in range(ST):
                        act.activation(probsT[:, s, :], turned[:, s, :], ACT.Copy).then_inc(probsT_ready, 1)

                def consume(u, pair):
                    name, part = UNITS[u]
                    act.wait_ge(tile_done, at(tile_done, l, tiles_for(u, pair)))
                    ps = pair_ps(u, pair)
                    if name == "xa":
                        ch = 4 * part + 2 * pair
                        act.activation(padded[:, ch:ch + 2, CONV_A_LEFT:CONV_A_LEFT + SEQ], ps, ACT.Copy).then_inc(bank_free[bank(u, pair)], 1)
                    elif name in ("q", "kv"):
                        i = 2 * (u - U["q", 0]) + pair
                        squares(i)
                    elif name == "xc":
                        if part == 1:
                            act.wait_ge(gated, at(gated, l, pair + 1))
                        act.activation(xc[:, 2 * pair:2 * pair + 2, :], ps, ACT.Copy).then_inc(bank_free[bank(u, pair)], 1)
                    elif name == "gc":
                        act.wait_ge(bank_free[bank(U["cc", part], pair)], freed_at(l, U["cc", part], pair))
                        act.activation(xc[:, 2 * pair:2 * pair + 2, :], ps, ACT.Sigmoid).then_inc(sigmoids, 1)
                    elif name in ("ga", "gb"):
                        silu_sigmoid((4 if name == "ga" else 8) + 2 * part + pair, u, pair)
                    elif name == "mg":
                        ch = 4 * (part % 2) + 2 * pair
                        act.activation(gates[:, ch:ch + 2, :], ps, ACT.Sigmoid).then_inc(bank_free[bank(u, pair)], 1)

                for k in range(CT):
                    act.wait_ge(x_gained, at(x_gained, l, k + 1))
                    act.activation(h_hi[:, k, :], buf_r[:, k, :], ACT.Identity,
                                   bias=mods[:, 0, k:k + 1]).then_inc(hhi_ready, 1)
                for n in range(FIRST_SPLITS, 4):
                    split_hi(l, n, last)

                for n in range(4, NT):
                    u, t = divmod(n, 4)
                    if n != MERGED_AT[-1]:
                        split_hi(l, n, last)
                    if UNITS[u - 1][0] == "rg":
                        act.wait_ge(tile_done, at(tile_done, l, 4 * (u - 1) + t + 1))
                        rg_sigmoids(UNITS[u - 1][1], t)
                    elif t % 2:
                        consume(u - 1, t // 2)
                    if n in (6, 8, 10, 12):
                        i = (n - 6) // 2
                        act.wait_ge(ua_ready, at(ua_ready, l, i + 1))
                        split_y(0, i, whole(ua), y_hi)
                    if n in (18, 22, 23):
                        q_norm({18: (0, 1), 22: (2, 3), 23: (4,)}[n])
                    if 28 <= n < 36:
                        rg_math(0, n - 28)
                    if 48 <= n < 56:
                        rg_math(1, n - 48)
                    if n in (64, 65, 66, 67):
                        act.wait_ge(gated, at(gated, l, n - 63))
                        split_y(1, n - 64, yc, y_hi)
                    if n in (72, 80, 88, 96):
                        softmax_exp((n - 72) // 8)
                    if n in (76, 84, 92, 100):
                        probs_out((n - 76) // 8)
                    if n in (82, 84, 86, 88):
                        i = (n - 82) // 2
                        act.wait_ge(gated, at(gated, l, 5 + i))
                        split_y(2, i, whole(ya), y_hi)
                    if n in (106, 108, 110, 112):
                        i = (n - 106) // 2
                        act.wait_ge(gated, at(gated, l, 9 + i))
                        split_y(3, i, whole(yb), y_hi)
                    if n in MERGED_AT:
                        i = MERGED_AT.index(n)
                        act.wait_ge(merged_ready, at(merged_ready, l, i + 1))
                        split_y(4, i, whole(merged), h_hi)
                    if n == MERGED_AT[-1]:
                        split_hi(l, n, last)
                    if n == NT - 2 and not last:
                        act.activation(warm[:], eps_col, ACT.Sqrt).then_inc(s_warm, 1)
                        square(l + 1, 0)
                if not last:
                    square(l + 1, 1)
                    for n in range(FIRST_SPLITS):
                        split_hi(l + 1, n)
                        square(l + 1, 2 + n)
                    root_mean_square(l + 1)
                assert own.n == S_STEPS, own.n

            with act.Fori(0, DEPTH - 1) as l:
                layer(l, False)
            layer(DEPTH - 1, True)

        @block.vector
        def _(vec):
            vec.memset(eps_col, EPS).then_inc(v_first, 1)
            vec.memset(ones, 1.0).then_inc(v_first, 1)
            vec.memset(padded[:, :, :], 0.0).then_inc(v_first, 1)
            vec.sem_inc(wlo_ready, NT)
            for b in range(BANKS):
                vec.sem_inc(bank_free[b], BANK_USES[b])

            def first_sum(a):
                if a < 3:
                    vec.wait_ge(raw_loaded[a], 16)
                    blocks = [raw[:, a, 512 * k:512 * k + 512] for k in range(8)]
                else:
                    blocks = [t[:, 2 * k:2 * k + 2, :].rearrange("p a b -> p (a b)") for t in (buf_t, ya) for k in range(4)]
                for k in range(8):
                    if a == 3 and k % 4 == 0:
                        vec.wait_ge(first_ada[k // 4], 16)
                    ck = par[:, 0, COL["c"] + k:COL["c"] + k + 1]
                    if k < 2:
                        ins = vec.tensor_scalar(blocks[k], blocks[k], ck, None, ALU.mult)
                    else:
                        vec.wait_ge(v_first, done[0] - 1)
                        ins = vec.scalar_tensor_tensor(out=blocks[k % 2], in0=blocks[k], scalar=ck, in1=blocks[k % 2],
                                                       op0=ALU.mult, op1=ALU.add)
                    ins.then_inc(v_first, 1)
                    done[0] += 1
                vec.wait_ge(v_first, done[0])
                vec.tensor_tensor(next_sums[a], blocks[0], blocks[1], ALU.add).then_inc(next_summed, 1)

            vec.wait_ge(params_loaded, 16)
            lam = par[:, :, COL["lru_lam"]:COL["lru_lam"] + 16]

            def scratch(i):
                return small[:, i, :].rearrange("p (a b) -> p a b", a=DEPTH)

            e_l, s_l, s2, q_l, sp = (scratch(i) for i in range(5))
            done = [3]

            def chain(instruction):
                instruction.then_inc(v_first, 1)
                done[0] += 1
                vec.wait_ge(v_first, done[0])

            vec.wait_ge(lam_exp, 2)
            chain(vec.tensor_scalar(s_l, e_l, 2.0, None, ALU.add))
            chain(vec.reciprocal(s_l, s_l))
            chain(vec.tensor_tensor(s_l, s_l, e_l, ALU.mult))
            chain(vec.tensor_tensor(s2, s_l, s_l, ALU.mult))
            chain(vec.tensor_scalar(q_l, s2, 1.0 / 15, None, ALU.mult))
            for odd in (13, 11, 9, 7, 5, 3):
                chain(vec.scalar_tensor_tensor(out=q_l, in0=q_l, scalar=1.0 / odd, in1=s2, op0=ALU.add, op1=ALU.mult))
            chain(vec.scalar_tensor_tensor(out=q_l, in0=q_l, scalar=1.0, in1=s_l, op0=ALU.add, op1=ALU.mult))
            chain(vec.tensor_scalar(sp, lam, -1.0, 0.0, ALU.mult, ALU.max))
            chain(vec.scalar_tensor_tensor(out=sp, in0=q_l, scalar=2.0, in1=sp, op0=ALU.mult, op1=ALU.add))
            for name, factor in (("pos8", LRU_C), ("neg8", -LRU_C), ("neg16", -2 * LRU_C)):
                chain(vec.tensor_scalar(par[:, :, COL[name]:COL[name] + 16], sp, factor, None, ALU.mult))
            for a in range(4):
                first_sum(a)

            def split_lo(l, n, last=False):
                t = n % 4
                vec.wait_ge(whi_ready, at(whi_ready, l, n + 1))
                vec.tensor_tensor(w_lo[:, t, :].rearrange("p (k m) -> p k m", k=8), raw_tile(n, RAW[last][0]),
                                  w_hi[:, t, :].bitcast(F32).rearrange("p (k m) -> p k m", k=8),
                                  ALU.subtract).then_inc(wlo_ready, 1)

            def input_factors(l):
                vec.tensor_copy(cur[:], par[:, bass.ds(l, 1), :].rearrange("p a b -> p (a b)")).then_inc(cur_ready, 1)
                vec.wait_ge(x_root, at(x_root, l, 1))
                vec.reciprocal(rstd[:], rstd[:]).then_inc(x_rstd, 1)
                vec.wait_ge(cur_ready, at(cur_ready, l, 1))
                vec.wait_ge(next_done, at(next_done, l, 1))
                vec.tensor_tensor(mods[:, 0:2, :], mod_ps[:, 0:16].rearrange("p (a b) -> p a b", a=2),
                                  cur[:, COL["b_ada"]:COL["b_ada"] + 16].rearrange("p (a b) -> p a b", a=2),
                                  ALU.add).then_inc(mods_ready, 1)
                vec.wait_ge(mods_ready, at(mods_ready, l, 1))
                vec.scalar_tensor_tensor(out=mods[:, 2, :], in0=mods[:, 1, :], scalar=1.0,
                                         in1=cur[:, COL["norm_g"]:COL["norm_g"] + 8], op0=ALU.add,
                                         op1=ALU.mult).then_inc(mods_ready, 1)

            input_factors(0)
            for n in range(FIRST_SPLITS):
                split_lo(0, n)

            def layer(l, last):
                own = Steps(v_step, l)

                def h_low(k):
                    vec.wait_ge(hhi_ready, at(hhi_ready, l, k + 1))
                    vec.scalar_tensor_tensor(out=h_lo[:, k, :], in0=buf_r[:, k, :], scalar=mods[:, 0, k:k + 1],
                                             in1=h_hi[:, k, :].bitcast(F32), op0=ALU.add,
                                             op1=ALU.subtract).then_inc(h_ready, 1)

                def gate():
                    vec.wait_ge(gate_done, at(gate_done, l, 1))
                    b = COL["b_ada"] + 16
                    vec.tensor_tensor(mods[:, 3, :], mod_ps[:, 16:24], cur[:, b:b + 8],
                                      ALU.add).then_inc(gate_ready, 1)

                def split_y(i, pair, src, hi, lo):
                    vec.wait_ge(yhi_ready, at(yhi_ready, l, PAIRS * i + pair + 1))
                    s = slice(2 * pair, 2 * pair + 2)
                    vec.tensor_tensor(lo[:, s, :], src(2 * pair, 2), hi[:, s, :].bitcast(F32),
                                      ALU.subtract).then_inc(y_ready, 1)

                def conv(pair, src, shift0, taps, weight, bias, dst, src_tile, signal=None):
                    chs = (2 * pair, 2 * pair + 1)
                    for k in range(taps):
                        for i, ch in enumerate(chs):
                            win = src[:, src_tile + i, shift0 + k:shift0 + k + SEQ]
                            col = COL[weight] + 8 * k + ch
                            wk = cur[:, col:col + 1]
                            if k == 0:
                                b = cur[:, COL[bias] + ch:COL[bias] + ch + 1] if bias else None
                                ins = vec.tensor_scalar(dst(ch, 1)[:, 0, :], win, wk, b, ALU.mult,
                                                        ALU.add if bias else ALU.bypass)
                            else:
                                vec.wait_ge(v_step, own.now(back=1))
                                ins = vec.scalar_tensor_tensor(out=dst(ch, 1)[:, 0, :], in0=win, scalar=wk,
                                                               in1=dst(ch, 1)[:, 0, :], op0=ALU.mult, op1=ALU.add)
                            if signal is not None and k == taps - 1 and i == 1:
                                ins.then_inc(signal, 1)
                            else:
                                ins.then_inc(v_step, own.next())

                def q_norm(i):
                    vec.wait_ge(q_rstd, at(q_rstd, l, i + 1))
                    g = COL["q_norm_g" if i < 4 else "k_norm_g"]
                    z = qkv[:, 2 * i:2 * i + 2, :]
                    vec.scalar_tensor_tensor(out=z, in0=z, scalar=cur[:, g:g + 1],
                                             in1=probs[:, 2 * (i % 2):2 * (i % 2) + 2, :], op0=ALU.mult,
                                             op1=ALU.mult).then_inc(q_normed, 1)

                def rope(i):
                    vec.wait_ge(q_rotated, at(q_rotated, l, i + 1))
                    z = qkv[:, 2 * i:2 * i + 2, :].rearrange("p a b -> p (a b)")
                    r = probsT[:, i % 2, :]
                    vec.tensor_tensor(r, turned[:, i % 2, :], sin2, ALU.mult).then_inc(v_step, own.next())
                    vec.tensor_tensor(z, z, cos2, ALU.mult).then_inc(v_step, own.next())
                    vec.wait_ge(v_step, own.now())
                    vec.tensor_tensor(z, z, r, ALU.add).then_inc(q_ready, 1)

                def rg_math(d, s):
                    if s in (0, 3):
                        half = s // 3
                        vec.wait_ge(bank_free[bank(U["rg", d], 4 + 2 * half + 1)], freed_at(l, U["rg", d], 4 + 2 * half + 1))
                        z = buf_i[:, 4 * half:4 * half + 4, :]
                        vec.tensor_tensor(z, z, ua_of(half), ALU.mult).then_inc(v_step, own.next())
                    if s in (2, 5):
                        half = (s - 2) // 3
                        vec.wait_ge(rg_exp, at(rg_exp, l, 2 * d + half + 1))
                        t4 = buf_t[:, 4 * half:4 * half + 4, :]
                        vec.scalar_tensor_tensor(out=t4.rearrange("p a b -> p (a b)"),
                                                 in0=tmp[:, :, :].rearrange("p a b -> p (a b)"), scalar=1.0,
                                                 in1=t4.rearrange("p a b -> p (a b)"), op0=ALU.add,
                                                 op1=ALU.mult).then_inc(rg_w, 1)
                    if s in (9, 10):
                        half = s - 9
                        vec.wait_ge(rg_root, at(rg_root, l, 2 * d + half + 1))
                        z = buf_i[:, 4 * half:4 * half + 4, :]
                        vec.tensor_tensor(z, z, buf_t[:, 4 * half:4 * half + 4, :], ALU.mult).then_inc(v_step, own.next())
                    if s in (11, 12):
                        half = s - 11
                        vec.wait_ge(v_step, own.now())
                        for j in range(4):
                            ch = 4 * half + j
                            a, u_, o = buf_r[:, ch, :], buf_i[:, ch, :], (ya if d == 0 else buf_t)[:, ch, :]
                            if d == 1:
                                a, u_, o = a[:, ::-1], u_[:, ::-1], o[:, ::-1]
                            ins = vec.tensor_tensor_scan(o, a, u_, 0.0, ALU.mult, ALU.add)
                            if j < 3:
                                ins.then_inc(v_step, own.next())
                            else:
                                ins.then_inc(scanned, 1)
                    if d == 1 and s in (13, 14):
                        half = s - 13
                        vec.wait_ge(scanned, at(scanned, l, 3 + half))
                        z = ya[:, 4 * half:4 * half + 4, :]
                        vec.tensor_tensor(z, z, buf_t[:, 4 * half:4 * half + 4, :], ALU.add).then_inc(v_step, own.next())

                def ua_of(half):
                    return ua[:, 4 * half:4 * half + 4, :]

                def silu_gate(i, u, pair, y, ch):
                    vec.wait_ge(sigmoids, at(sigmoids, l, i + 1))
                    z = xc[:, 2 * (i % 2):2 * (i % 2) + 2, :]
                    vec.tensor_tensor(z, z, pair_ps(u, pair), ALU.mult).then_inc(bank_free[bank(u, pair)], 1)
                    vec.wait_ge(bank_free[bank(u, pair)], freed_at(l, u, pair))
                    vec.tensor_tensor(y(ch, 2), y(ch, 2), z, ALU.mult).then_inc(gated, 1)

                def softmax_max(g):
                    vec.wait_ge(scored, at(scored, l, g + 1))
                    vec.tensor_reduce(stat[:, 0, :], scores[:, :, :], AX_X, ALU.max).then_inc(v_step, own.next())
                    vec.wait_ge(v_step, own.now())
                    vec.tensor_scalar(stat[:, 1, :], stat[:, 0, :], -SCALE, None, ALU.mult).then_inc(max_ready, 1)

                def softmax_norm(g):
                    vec.wait_ge(exp_done, at(exp_done, l, g + 1))
                    vec.reciprocal(stat[:, 3, :], stat[:, 2, :]).then_inc(v_step, own.next())
                    vec.wait_ge(v_step, own.now())
                    for j in range(4):
                        ins = vec.tensor_scalar(probs[:, j, :], probs[:, j, :], stat[:, 3, j:j + 1], None, ALU.mult)
                        if j < 3:
                            ins.then_inc(v_step, own.next())
                    ins.then_inc(probs_ready, 1)

                def consume(u, pair):
                    name, part = UNITS[u]
                    ps = pair_ps(u, pair)
                    if name == "xa":
                        vec.wait_ge(bank_free[bank(u, pair)], freed_at(l, u, pair))
                        ch = 4 * part + 2 * pair
                        conv(ch // 2, padded, 0, CONV_A_W, "conv_a_w", "conv_a_b", whole(ua), ch, signal=ua_ready)
                    elif name == "cc":
                        vec.wait_ge(tile_done, at(tile_done, l, tiles_for(u, pair)))
                        vec.wait_ge(bank_free[bank(U["xc", part], pair)], freed_at(l, U["xc", part], pair))
                        vec.tensor_tensor(padded[:, 2 * pair:2 * pair + 2, CONV_A_LEFT:CONV_A_LEFT + SEQ], ps,
                                                xc[:, 2 * pair:2 * pair + 2, :], ALU.mult).then_inc(bank_free[bank(u, pair)], 1)
                    elif name == "bc":
                        vec.wait_ge(tile_done, at(tile_done, l, tiles_for(u, pair)))
                        vec.wait_ge(v_step, own.now())
                        ch = 4 * part + 2 * pair
                        vec.tensor_tensor(yc(ch, 2), yc(ch, 2), ps, ALU.mult).then_inc(bank_free[bank(u, pair)], 1)
                    elif name == "gc":
                        silu_gate(2 * part + pair, u, pair, yc, 4 * part + 2 * pair)
                    elif name == "ga":
                        silu_gate(4 + 2 * part + pair, u, pair, whole(ya), 4 * part + 2 * pair)
                    elif name == "gb":
                        silu_gate(8 + 2 * part + pair, u, pair, whole(yb), 4 * part + 2 * pair)
                    elif name == "br":
                        branch, half = divmod(part, 2)
                        ch = 4 * half + 2 * pair
                        vec.wait_ge(tile_done, at(tile_done, l, tiles_for(u, pair)))
                        vec.wait_ge(bank_free[bank(U["mg", part], pair)], freed_at(l, U["mg", part], pair))
                        m, g = merged[:, ch:ch + 2, :], gates[:, ch:ch + 2, :]
                        if branch == BR_C:
                            vec.tensor_tensor(m, g, ps, ALU.mult).then_inc(bank_free[bank(u, pair)], 1)
                        else:
                            z = tmp[:, 2 * pair:2 * pair + 2, :]
                            vec.tensor_tensor(z, g, ps, ALU.mult).then_inc(bank_free[bank(u, pair)], 1)
                            vec.wait_ge(bank_free[bank(u, pair)], freed_at(l, u, pair))
                            ins = vec.tensor_tensor(m, m, z, ALU.add)
                            if branch == BR_B:
                                ins.then_inc(merged_ready, 1)
                            else:
                                ins.then_inc(v_step, own.next())
                    elif name == "out":
                        vec.wait_ge(tile_done, at(tile_done, l, tiles_for(u, pair)))
                        vec.wait_ge(gate_ready, at(gate_ready, l, 1))
                        for i in range(2):
                            ch = 4 * part + 2 * pair + i
                            ins = vec.scalar_tensor_tensor(out=xT[:, ch, :], in0=ps[:, i, :],
                                                           scalar=mods[:, 3, ch:ch + 1], in1=xT[:, ch, :],
                                                           op0=ALU.mult, op1=ALU.add)
                            if i == 0:
                                ins.then_inc(v_step, own.next())
                        ins.then_inc(bank_free[bank(u, pair)], 1)

                vec.wait_ge(x_rstd, at(x_rstd, l, 1))
                vec.wait_ge(mods_ready, at(mods_ready, l, 2))
                for k in range(CT):
                    vec.scalar_tensor_tensor(out=buf_r[:, k, :], in0=xT[:, k, :], scalar=mods[:, 2, k:k + 1],
                                             in1=rstd[:], op0=ALU.mult, op1=ALU.mult).then_inc(x_gained, 1)
                    if k >= 1:
                        h_low(k - 1)
                h_low(CT - 1)
                for n in range(FIRST_SPLITS, 4):
                    split_lo(l, n, last)

                for n in range(4, NT):
                    u, t = divmod(n, 4)
                    if n != MERGED_AT[-1]:
                        split_lo(l, n, last)
                    if UNITS[u - 1][0] != "rg" and t % 2:
                        consume(u - 1, t // 2)
                    if n in (6, 8, 10, 12):
                        split_y(0, (n - 6) // 2, whole(ua), y_hi, y_lo)
                    if n in (18, 22):
                        q_norm((n - 18) // 2)
                        q_norm((n - 18) // 2 + 1)
                    if n == 23:
                        q_norm(4)
                    if n in ROPE_AT:
                        rope(ROPE_AT.index(n))
                    if n == GATE_AT + 4:
                        gate()
                    if n == V_COPY_AT:
                        vec.wait_ge(v_turned, at(v_turned, l, 1))
                        vec.tensor_copy(vtok[:, :, :, :].rearrange("p a b c -> p (a b c)"),
                                        turned[:, 1, :]).then_inc(v_ready, 1)
                    for d, start in ((0, 28), (1, 48)):
                        if start <= n < start + 15:
                            rg_math(d, n - start)
                    for part, start in ((0, 34), (1, 54)):
                        if n in (start, start + 2):
                            pair = (n - start) // 2
                            vec.wait_ge(bank_free[bank(U["cc", part], pair)], freed_at(l, U["cc", part], pair))
                            conv(2 * part + pair, padded, CONV_A_LEFT - CONV_C_LEFT, CONV_C_W, "conv_c_w", None,
                                 yc, 2 * pair)
                    if n in (64, 65, 66, 67):
                        split_y(1, n - 64, yc, y_hi, y_lo)
                    if n in (72, 80, 88, 96):
                        softmax_max((n - 72) // 8)
                    if n in (73, 81, 89, 97):
                        softmax_norm((n - 73) // 8)
                    if n in (80, 88, 96, 104):
                        g = (n - 80) // 8
                        vec.wait_ge(o_summed, at(o_summed, l, g + 1))
                        vec.tensor_copy(yb[:, 2 * g:2 * g + 2, :],
                                        turned[:, 0, :].rearrange("p (a b) -> p a b", a=2)).then_inc(o_ready, 1)
                    if n in (82, 84, 86, 88):
                        split_y(2, (n - 82) // 2, whole(ya), y_hi, y_lo)
                    if n in (106, 108, 110, 112):
                        split_y(3, (n - 106) // 2, whole(yb), y_hi, y_lo)
                    if n in MERGED_AT:
                        split_y(4, MERGED_AT.index(n), whole(merged), h_hi, h_lo)
                    if n == MERGED_AT[-1]:
                        split_lo(l, n, last)
                consume(NU - 1, 0)
                if not last:
                    for n in range(FIRST_SPLITS):
                        split_lo(l + 1, n)
                consume(NU - 1, 1)
                if not last:
                    input_factors(l + 1)
                assert own.n == V_STEPS, own.n

            with vec.Fori(0, DEPTH - 1) as l:
                layer(l, False)
            layer(DEPTH - 1, True)

        @block.gpsimd
        def _(pool):
            pool.wait_ge(params_loaded, 16)
            pool.wait_ge(raw_loaded[0], 48)
            pool.dma_start(cst[:], consts).then_inc(consts_loaded, 16)

            def layer(l, last):
                slot_of, raw_ready = RAW[last][:2]
                own = Steps(p_step, l)
                for a in [i for kind, i in PLAN[last] if kind == "ada"]:
                    slot = slot_of["ada", a]
                    w = raw[:, slot, :]
                    pool.wait_ge(raw_loaded[slot], at(raw_loaded[slot], l, raw_ready["ada", a]))
                    for k in range(8):
                        col = COL["c"] + k
                        pool.tensor_scalar(w[:, 512 * k:512 * k + 512], w[:, 512 * k:512 * k + 512],
                                           par[:, 0, col:col + 1], 1.0, ALU.mult, ALU.mult).then_inc(p_step, own.next())
                    for half in (2048, 1024):
                        pool.wait_ge(p_step, own.now())
                        pool.tensor_tensor(w[:, 0:half], w[:, 0:half], w[:, half:2 * half],
                                           ALU.add).then_inc(p_step, own.next())
                    pool.wait_ge(p_step, own.now())
                    if a >= 4:
                        pool.wait_ge(q_ready, at(q_ready, l, 5))
                        pool.tensor_tensor(gate_sums[a - 4], w[:, 0:512], w[:, 512:1024],
                                           ALU.add).then_inc(gate_summed, 1)
                    else:
                        pool.wait_ge(scored, at(scored, l, 4))
                        pool.tensor_tensor(next_sums[a], w[:, 0:512], w[:, 512:1024],
                                           ALU.add).then_inc(next_summed, 1)

            with pool.Fori(0, DEPTH - 1) as l:
                layer(l, False)
            layer(DEPTH - 1, True)

        @block.tensor
        def _(pe):
            pe.sem_inc(tile_done, NT)

            def column_sums(w, col):
                for t in range(4):
                    ins = pe.matmul(mod_ps[:, col + t:col + t + 1], w[:, P * t:P * (t + 1)], ones[:, 0:1],
                                    start=True, stop=True)
                return ins

            def square_sums(l, pairs):
                for pair in pairs:
                    pe.wait_ge(x_squared, at(x_squared, l, pair + 1))
                    for k in (2 * pair, 2 * pair + 1):
                        ins = pe.matmul(scores[:, 0, :], ones, buf_i[:, k, :], start=k == 0, stop=k == CT - 1)
                if PAIRS - 1 in pairs:
                    ins.then_inc(x_summed, 1)

            def shift_scale(l, units):
                for a in units:
                    pe.wait_ge(next_summed, at(next_summed, l, a + 1))
                    ins = column_sums(next_sums[a], 4 * a)
                if 3 in units:
                    ins.then_inc(next_done, 1)

            pe.wait_ge(v_first, 2)
            shift_scale(0, (0, 1))
            square_sums(0, range(PAIRS))
            shift_scale(0, (2, 3))

            def layer(l, last):
                def three(ps, n, blk, hi, lo, first, last):
                    t = n % 4
                    wh = w_hi[:, t, P * blk:P * (blk + 1)]
                    wl = w_lo[:, t, P * blk:P * (blk + 1)]
                    pe.matmul(ps, wh, hi, start=first, stop=False)
                    pe.matmul(ps, wh, lo, start=False, stop=False)
                    return pe.matmul(ps, wl, hi, start=False, stop=last)

                def bank_wait(u, i):
                    b, use = BANK[u, i]
                    pe.wait_ge(bank_free[b], at(bank_free[b], l, use))

                def product(n, hi, lo, ready=None, per=1, base=0):
                    u, t = place(n)
                    pe.wait_ge(wlo_ready, at(wlo_ready, l, n + 1))
                    if t % 2 == 0:
                        bank_wait(u, t // 2)
                    ps = pair_ps(u, t // 2)[:, t % 2, :]
                    for k in range(CT):
                        if ready is not None and k % per == 0:
                            pe.wait_ge(ready, at(ready, l, base + k // per + 1))
                        ins = three(ps, n, k, hi[:, k, :], lo[:, k, :], k == 0, k == CT - 1)
                    ins.then_inc(tile_done, 1)

                def first_products():
                    pe.wait_ge(wlo_ready, at(wlo_ready, l, 2))
                    bank_wait(0, 0)
                    bank_wait(0, 1)
                    for k in range(CT):
                        pe.wait_ge(h_ready, at(h_ready, l, k + 1))
                        for n in range(2):
                            ins = three(pair_ps(0, n)[:, 0, :], n, k, h_hi[:, k, :], h_lo[:, k, :], k == 0, k == CT - 1)
                            if k == CT - 1:
                                ins.then_inc(tile_done, 1)

                def rg_product(n):
                    u, t = divmod(n, 4)
                    half = t % 2
                    pe.wait_ge(wlo_ready, at(wlo_ready, l, n + 1))
                    for j in range(4):
                        if j % 2 == 0:
                            bank_wait(u, 2 * t + j // 2)
                        blk2, m = divmod(j, 2)
                        ps = pair_ps(u, 2 * t + j // 2)[:, j % 2, :]
                        for kt in range(2):
                            k = 4 * half + 2 * blk2 + kt
                            ins = three(ps, n, 4 * blk2 + 2 * kt + m, y_hi[:, k, :], y_lo[:, k, :], kt == 0, kt == 1)
                    ins.then_inc(tile_done, 1)

                def q_sum(i):
                    pe.wait_ge(q_squared, at(q_squared, l, i + 1))
                    if i >= 2:
                        pe.wait_ge(q_rstd, at(q_rstd, l, i - 1))
                    sq = tmp[:, 2 * (i % 2):2 * (i % 2) + 2, :].rearrange("p a b -> p (a b)")
                    pe.matmul(sums[i % 2], ones, sq, start=True, stop=True).then_inc(q_summed, 1)

                def q_rotate(i):
                    pe.wait_ge(q_normed, at(q_normed, l, i + 1))
                    if i == 0:
                        pe.wait_ge(consts_loaded, 16)
                    if i >= 2:
                        pe.wait_ge(q_ready, at(q_ready, l, i - 1))
                    pe.matmul(turned[:, i % 2, :], rot, qkv[:, 2 * i:2 * i + 2, :].rearrange("p a b -> p (a b)"),
                              start=True, stop=True).then_inc(q_rotated, 1)

                def v_turn():
                    pe.wait_ge(bank_free[bank(U["kv", 0], 1)], freed_at(l, U["kv", 0], 1))
                    pe.wait_ge(q_ready, at(q_ready, l, 4))
                    for s in range(ST):
                        for j in range(N_KV):
                            o = (N_KV * s + j) * HD
                            ins = pe.transpose(turned[:, 1, o:o + HD], qkv[:, 10 + j, P * s:P * (s + 1)], ident)
                    ins.then_inc(v_turned, 1)

                def gate():
                    for i in range(2):
                        pe.wait_ge(gate_summed, at(gate_summed, l, i + 1))
                        ins = column_sums(gate_sums[i], 16 + 4 * i)
                    ins.then_inc(gate_done, 1)

                def attention_scores(g):
                    if g == 0:
                        pe.wait_ge(q_ready, at(q_ready, l, 5))
                        pe.wait_ge(gate_ready, at(gate_ready, l, 1))
                    else:
                        pe.wait_ge(exp_done, at(exp_done, l, g))
                    for i in range(2):
                        for s in range(ST):
                            ins = pe.matmul(scores[:, 2 * i + s, :], qkv[:, 2 * g + i, P * s:P * (s + 1)],
                                            qkv[:, 8 + g // 2, :], start=True, stop=True)
                    ins.then_inc(scored, 1)

                def attention_turn(g):
                    pe.wait_ge(probs_ready, at(probs_ready, l, g + 1))
                    if g == 0:
                        pe.wait_ge(v_ready, at(v_ready, l, 1))
                    else:
                        pe.wait_ge(o_ready, at(o_ready, l, g))
                    for s in range(ST):
                        for i in range(2):
                            for qs in range(ST):
                                o = SEQ * i + P * qs
                                ins = pe.transpose(turned[:, s, o:o + P], probs[:, 2 * i + qs, P * s:P * (s + 1)], ident)
                    ins.then_inc(probs_turned, 1)

                def attention_out(g):
                    pe.wait_ge(probsT_ready, at(probsT_ready, l, 2 * g + 2))
                    for s in range(ST):
                        ins = pe.matmul(turned[:, 0, :], vtok[:, s, g // 2, :], probsT[:, s, :], start=s == 0,
                                        stop=s == ST - 1)
                    ins.then_inc(o_summed, 1)

                first_products()
                for n in range(2, NT):
                    u, t = divmod(n, 4)
                    name, part = UNITS[u]
                    if n in Q_SUM_AT:
                        q_sum(Q_SUM_AT.index(n))
                    if n in Q_ROTATE_AT:
                        q_rotate(Q_ROTATE_AT.index(n))
                    if n == V_TURN_AT:
                        v_turn()
                    if n in (68, 76, 84, 92):
                        attention_scores((n - 68) // 8)
                    if n in (73, 81, 89, 97):
                        attention_turn((n - 73) // 8)
                    if n in (76, 84, 92, 100):
                        attention_out((n - 76) // 8)
                    if n == GATE_AT:
                        gate()
                    if n == NT - 1 and not last:
                        square_sums(l + 1, (0, 1, 2))
                    if name == "rg":
                        if n == 4 * U["rg", 0]:
                            pe.wait_ge(y_ready, at(y_ready, l, PAIRS))
                        rg_product(n)
                    elif name == "br":
                        first = t == 0 and part % 2 == 0
                        i = {BR_C: 1, BR_A: 2, BR_B: 3}[part // 2]
                        product(n, y_hi, y_lo, y_ready if first else None, 2, PAIRS * i)
                    elif name == "out":
                        product(n, h_hi, h_lo, y_ready if n == 4 * U_OUT else None, 2, PAIRS * 4)
                    else:
                        product(n, h_hi, h_lo)
                if not last:
                    shift_scale(l + 1, (0, 1))
                    square_sums(l + 1, (3,))
                    shift_scale(l + 1, (2, 3))

            with pe.Fori(0, DEPTH - 1) as l:
                layer(l, False)
            layer(DEPTH - 1, True)


def shape_constants():
    k = np.zeros((P, N_CONST), np.float32)
    k[:, C_ID:C_ID + P] = np.eye(P, dtype=np.float32)
    for m in range(P):
        if m % 64 < 32:
            k[m + 32, C_ROT + m] = -1.0
        else:
            k[m - 32, C_ROT + m] = 1.0
    half = HD // 2
    inv = (np.float32(ROPE_THETA) ** (-np.arange(0, half, 2, dtype=np.float32) / np.float32(half))).astype(np.float32)
    tok = np.arange(SEQ)
    for p in range(P):
        at = (tok // GRID_W if p < half else tok % GRID_W).astype(np.float32)
        ang = (at * inv[p % 32]).astype(np.float32)
        for r in range(2):
            k[p, C_COS + SEQ * r:C_COS + SEQ * (r + 1)] = np.cos(ang)
            k[p, C_SIN + SEQ * r:C_SIN + SEQ * (r + 1)] = np.sin(ang)
    return k


def packed_params(inputs):
    rows = []
    for layer in range(DEPTH):
        for name, n in PARAMS.items():
            a = inputs[name][0] if name == "c" else inputs[name][layer]
            rows.append(np.reshape(a, (n, P)))
    return np.ascontiguousarray(np.concatenate(rows).reshape(DEPTH, N_ROWS, P).transpose(2, 0, 1))


def kernel(**inputs):
    import concourse.bacc as bacc
    from concourse.bass_utils import run_bass_kernel_spmd

    inputs = {name: np.asarray(a) for name, a in inputs.items()}
    nc = bacc.Bacc("TRN2", target_bir_lowering=False, num_devices=1)
    arrays = {name: np.ascontiguousarray(inputs[name]) for name in ("w_ada", "w_in", "w_rg", "w_ig", "w_branch", "w_out")}
    arrays["x"] = np.ascontiguousarray(inputs["x"][0].reshape(SEQ, CT, P).transpose(2, 1, 0))
    arrays["params"] = packed_params(inputs)
    arrays["consts"] = shape_constants()
    args = [nc.dram_tensor(f"in_{n}", a.shape, mybir.dt.from_np(a.dtype), kind="ExternalInput").ap()
            for n, a in arrays.items()]
    out = nc.dram_tensor("out", (P, CT, SEQ), F32, kind="ExternalOutput").ap()
    trunk_program(nc, *args, out)
    result = run_bass_kernel_spmd(nc, [{f"in_{n}": a for n, a in arrays.items()}], core_ids=[0])
    return np.ascontiguousarray(result.results[0]["out"].transpose(2, 1, 0)).reshape(1, SEQ, D)
```
